# Optimizing a Trainium2 kernel written in Bass

```python
import jax
import jax.numpy as jnp
from jax import lax
import numpy as np
import math

D_MODEL = 1024
BATCH = 1
SEQ = 256
DEPTH = 2

N_HEADS = 16
HEAD_DIM = D_MODEL // N_HEADS
N_KV_GROUPS = 4
HEADS_PER_GROUP = N_HEADS // N_KV_GROUPS
N_BRANCH = 3
CMP_LEN = 32
CMP_STRIDE = 16
CMP_HIDDEN = 4 * HEAD_DIM
SLC_LEN = 64
SLC_TOP_N = 16
WINDOW = 512
Q_BLOCK = 64
D_FF = 2816
CONV_WIDTH = 3
RMS_EPS = 1e-6
NEG_INF = -1e30
FORCE_SCORE = 1e30


def rms_norm(x, g):
    x32 = x.astype(jnp.float32)
    y = x32 * lax.rsqrt(jnp.mean(x32 * x32, axis=-1, keepdims=True) + RMS_EPS)
    return (y * g.astype(jnp.float32)).astype(x.dtype)

def masked_softmax(s, mask):
    s = jnp.where(mask, s, NEG_INF)
    m = jnp.max(s, axis=-1, keepdims=True)
    e = jnp.where(mask, jnp.exp(s - m), 0.0)
    return e / jnp.maximum(jnp.sum(e, axis=-1, keepdims=True), 1e-30)

def alibi_slopes():
    h = jnp.arange(1, N_HEADS + 1, dtype=jnp.float32)
    return jnp.exp2(-8.0 * h / N_HEADS).reshape(N_KV_GROUPS, HEADS_PER_GROUP)

def modulate_pre(x, g_pre, shift, scale):
    return rms_norm(x, g_pre) * (1.0 + scale[:, None, :]) + shift[:, None, :]

def gated_post_add(x, y, g_post, gate, weight):
    return x + weight * gate[:, None, :] * rms_norm(y, g_post)

def swiglu_ffn(h, w_in, w_out):
    g, u = jnp.split(h @ w_in, 2, axis=-1)
    return (jax.nn.silu(g) * u) @ w_out

def causal_shift(v, n):
    if n == 0:
        return v
    return jnp.pad(v[:, :-n], ((0, 0), (n, 0), (0, 0)))

def short_conv_mixer(h, w_in, conv_w, w_out):
    b_gate, c_gate, u = jnp.split(h @ w_in, 3, axis=-1)
    v = c_gate * u
    y = sum(conv_w[k] * causal_shift(v, CONV_WIDTH - 1 - k) for k in range(CONV_WIDTH))
    return (b_gate * y) @ w_out

def build_shared_kv(x, c, kv_norm_g, kv_ada_w, kv_ada_b, kv_w, cmp_pos, cmp_w1, cmp_w2):
    B, S, _ = x.shape
    G, dh = N_KV_GROUPS, HEAD_DIM
    shift, scale = jnp.split(jax.nn.silu(c) @ kv_ada_w + kv_ada_b, 2, axis=-1)
    h = modulate_pre(x, kv_norm_g, shift, scale)
    kv = (h @ kv_w).reshape(B, S, N_BRANCH, 2, G, dh)
    kv = jnp.transpose(kv, (2, 3, 0, 4, 1, 5))
    n_cmp = (S - CMP_LEN) // CMP_STRIDE + 1
    tok = jnp.arange(n_cmp)[:, None] * CMP_STRIDE + jnp.arange(CMP_LEN)[None, :]
    blocks = kv[0][:, :, :, tok] + cmp_pos[:, None, None, None]
    blocks = blocks.reshape(2, B, G, n_cmp, CMP_LEN * dh)
    hid = jax.nn.gelu(jnp.einsum('kbgnf,kfh->kbgnh', blocks, cmp_w1))
    kv_cmp = jnp.einsum('kbgnh,khd->kbgnd', hid, cmp_w2)
    kv_slc = kv[1].reshape(2, B, G, S // SLC_LEN, SLC_LEN, dh)
    kv_win = jnp.pad(kv[2], ((0, 0), (0, 0), (0, 0), (WINDOW, 0), (0, 0)))
    return kv_cmp, kv_slc, kv_win

def nsa_mixer(h, kv_cmp, kv_slc, kv_win, w_in, w_out):
    B, S, _ = h.shape
    G, R, dh = N_KV_GROUPS, HEADS_PER_GROUP, HEAD_DIM
    f32 = jnp.float32
    proj = h @ w_in
    q = proj[..., :N_HEADS * dh].reshape(B, S, G, R, dh) * (dh ** -0.5)
    gates = jax.nn.sigmoid(proj[..., N_HEADS * dh:].astype(f32)).reshape(B, S, N_BRANCH, G, R)
    k_cmp, v_cmp = kv_cmp[0], kv_cmp[1]
    k_slc, v_slc = kv_slc[0], kv_slc[1]
    k_win, v_win = kv_win[0], kv_win[1]
    n_cmp = k_cmp.shape[2]
    n_slc = k_slc.shape[2]
    top_n = min(SLC_TOP_N, n_slc)
    cmp_start = jnp.arange(n_cmp) * CMP_STRIDE
    cmp_end = cmp_start + CMP_LEN - 1
    slc_start = jnp.arange(n_slc) * SLC_LEN
    overlap = ((cmp_start[:, None] < slc_start[None, :] + SLC_LEN)
               & (cmp_end[:, None] >= slc_start[None, :])).astype(f32)
    slopes = alibi_slopes()
    sl5 = slopes[None, :, :, None, None]
    bi = jnp.arange(B)[:, None, None, None]
    gi = jnp.arange(G)[None, :, None, None]
    blk = jnp.arange(n_slc)

    def attend_block(qi):
        q0 = qi * Q_BLOCK
        qb = lax.dynamic_slice_in_dim(q, q0, Q_BLOCK, axis=1)
        t = q0 + jnp.arange(Q_BLOCK)
        d_cmp = t[:, None] - cmp_end[None, :]
        s = jnp.einsum('bqgrd,bgnd->bgrqn', qb, k_cmp, preferred_element_type=f32)
        s = s - sl5 * d_cmp.astype(f32)
        p_cmp = masked_softmax(s, d_cmp >= 0)
        o_cmp = jnp.einsum('bgrqn,bgnd->bqgrd', p_cmp.astype(v_cmp.dtype), v_cmp)
        imp = jnp.einsum('bgrqn,nj->bgqj', p_cmp, overlap)
        cur = t // SLC_LEN
        forced = (blk[None, :] == 0) | (blk[None, :] == cur[:, None]) | (blk[None, :] == cur[:, None] - 1)
        future = slc_start[None, :] > t[:, None]
        imp = jnp.where(forced, FORCE_SCORE, jnp.where(future, NEG_INF, imp))
        _, idx = lax.top_k(imp, top_n)
        k_sel = k_slc[bi, gi, idx]
        v_sel = v_slc[bi, gi, idx]
        d_sel = t[None, None, :, None, None] - (idx[..., None] * SLC_LEN + jnp.arange(SLC_LEN))
        s = jnp.einsum('bqgrd,bgqnld->bgrqnl', qb, k_sel, preferred_element_type=f32)
        s = s - slopes[None, :, :, None, None, None] * d_sel[:, :, None].astype(f32)
        s = s.reshape(B, G, R, Q_BLOCK, top_n * SLC_LEN)
        m_sel = (d_sel >= 0)[:, :, None].reshape(B, G, 1, Q_BLOCK, top_n * SLC_LEN)
        p_sel = masked_softmax(s, m_sel).reshape(B, G, R, Q_BLOCK, top_n, SLC_LEN)
        o_sel = jnp.einsum('bgrqnl,bgqnld->bqgrd', p_sel.astype(v_sel.dtype), v_sel)
        kw = lax.dynamic_slice_in_dim(k_win, q0, WINDOW + Q_BLOCK, axis=2)
        vw = lax.dynamic_slice_in_dim(v_win, q0, WINDOW + Q_BLOCK, axis=2)
        spos = q0 - WINDOW + jnp.arange(WINDOW + Q_BLOCK)
        d_win = t[:, None] - spos[None, :]
        m_win = (d_win >= 0) & (d_win < WINDOW) & (spos[None, :] >= 0)
        s = jnp.einsum('bqgrd,bgkd->bgrqk', qb, kw, preferred_element_type=f32)
        s = s - sl5 * d_win.astype(f32)
        p_win = masked_softmax(s, m_win)
        o_win = jnp.einsum('bgrqk,bgkd->bqgrd', p_win.astype(vw.dtype), vw)
        g = lax.dynamic_slice_in_dim(gates, q0, Q_BLOCK, axis=1)
        o = (g[:, :, 0, :, :, None] * o_cmp.astype(f32)
             + g[:, :, 1, :, :, None] * o_sel.astype(f32)
             + g[:, :, 2, :, :, None] * o_win.astype(f32))
        return o.astype(h.dtype)

    o = lax.map(attend_block, jnp.arange(S // Q_BLOCK))
    o = jnp.moveaxis(o, 0, 1).reshape(B, S, N_HEADS * dh)
    return o @ w_out

def first_inputs(seed: int = 0) -> dict:
    key = jax.random.key(seed)
    ks = jax.random.split(key, 20)
    f32 = jnp.float32
    D = D_MODEL
    n_a = DEPTH // 2
    n_b = DEPTH - n_a
    kv_cols = N_BRANCH * 2 * N_KV_GROUPS * HEAD_DIM

    def dense(k, shape, fan_in):
        return jax.random.normal(k, shape, f32) * fan_in ** -0.5

    def small(k, shape, s):
        return jax.random.normal(k, shape, f32) * s

    return {
        "x": jax.random.normal(ks[0], (BATCH, SEQ, D), f32),
        "c": jax.random.normal(ks[1], (BATCH, D), f32),
        "ada_w": dense(ks[2], (DEPTH, D, 9 * D), D),
        "ada_b": small(ks[3], (DEPTH, 9 * D), 0.01),
        "norm_g": 1.0 + small(ks[4], (DEPTH, 3, 2, D), 0.05),
        "ffn_w_in": dense(ks[5], (DEPTH, 2, D, 2 * D_FF), D),
        "ffn_w_out": dense(ks[6], (DEPTH, 2, D_FF, D), D_FF),
        "a_w_in": dense(ks[7], (n_a, D, 3 * D), D),
        "a_conv": dense(ks[8], (n_a, CONV_WIDTH, D), CONV_WIDTH),
        "a_w_out": dense(ks[9], (n_a, D, D), D),
        "kv_norm_g": 1.0 + small(ks[10], (D,), 0.05),
        "kv_ada_w": dense(ks[11], (D, 2 * D), D),
        "kv_ada_b": small(ks[12], (2 * D,), 0.01),
        "kv_w": dense(ks[13], (D, kv_cols), D),
        "cmp_pos": small(ks[14], (2, CMP_LEN, HEAD_DIM), 0.1),
        "cmp_w1": dense(ks[15], (2, CMP_LEN * HEAD_DIM, CMP_HIDDEN), CMP_LEN * HEAD_DIM),
        "cmp_w2": dense(ks[16], (2, CMP_HIDDEN, HEAD_DIM), CMP_HIDDEN),
        "b_w_in": dense(ks[17], (n_b, D, N_HEADS * HEAD_DIM + N_BRANCH * N_HEADS), D),
        "b_w_out": dense(ks[18], (n_b, N_HEADS * HEAD_DIM, D), N_HEADS * HEAD_DIM),
    }

def first_block(x, c, ada_w, ada_b, norm_g, ffn_w_in, ffn_w_out, a_w_in, a_conv, a_w_out,
              kv_norm_g, kv_ada_w, kv_ada_b, kv_w, cmp_pos, cmp_w1, cmp_w2, b_w_in, b_w_out):
    B = x.shape[0]
    D = x.shape[-1]
    n_a = DEPTH // 2
    kv_cmp = kv_slc = kv_win = None
    for layer in range(DEPTH):
        if layer == n_a:
            kv_cmp, kv_slc, kv_win = build_shared_kv(
                x, c, kv_norm_g, kv_ada_w, kv_ada_b, kv_w, cmp_pos, cmp_w1, cmp_w2)
        mod = (jax.nn.silu(c) @ ada_w[layer] + ada_b[layer]).reshape(B, 3, 3, D)
        g = norm_g[layer]
        h = modulate_pre(x, g[0, 0], mod[:, 0, 0], mod[:, 0, 1])
        y = swiglu_ffn(h, ffn_w_in[layer, 0], ffn_w_out[layer, 0])
        x = gated_post_add(x, y, g[0, 1], mod[:, 0, 2], 0.5)
        h = modulate_pre(x, g[1, 0], mod[:, 1, 0], mod[:, 1, 1])
        if layer < n_a:
            y = short_conv_mixer(h, a_w_in[layer], a_conv[layer], a_w_out[layer])
        else:
            y = nsa_mixer(h, kv_cmp, kv_slc, kv_win, b_w_in[layer - n_a], b_w_out[layer - n_a])
        x = gated_post_add(x, y, g[1, 1], mod[:, 1, 2], 1.0)
        h = modulate_pre(x, g[2, 0], mod[:, 2, 0], mod[:, 2, 1])
        y = swiglu_ffn(h, ffn_w_in[layer, 1], ffn_w_out[layer, 1])
        x = gated_post_add(x, y, g[2, 1], mod[:, 2, 2], 0.5)
    return x


GRID_W = 64
CTX_LEN = 256
N_MIXERS = 3
Q_BLOCK_2 = 128
ROPE_BASE = 10000.0
NORM_EPS = 1e-6

DIFF_DH = 64
DIFF_HEADS = D_MODEL // (2 * DIFF_DH)
GQA_DH = 128
GQA_HEADS = D_MODEL // GQA_DH
GQA_KV_HEADS = max(GQA_HEADS // 4, 1)
GQA_GROUP = GQA_HEADS // GQA_KV_HEADS
GLA_HEADS = 4
GLA_DK = D_MODEL // 2
GLA_DV = D_MODEL
GLA_DK_H = GLA_DK // GLA_HEADS
GLA_DV_H = GLA_DV // GLA_HEADS
GLA_GATE_RANK = 16
GLA_TAU = 16.0
GLA_CHUNK = 64
FFN_HIDDEN = ((8 * D_MODEL // 3 + 255) // 256) * 256

N_A = len(range(0, DEPTH, N_MIXERS))
N_B = len(range(1, DEPTH, N_MIXERS))
N_C = len(range(2, DEPTH, N_MIXERS))


def rmsnorm(x, g):
    x32 = x.astype(jnp.float32)
    y = x32 * lax.rsqrt(jnp.mean(x32 * x32, axis=-1, keepdims=True) + NORM_EPS)
    return (y * g.astype(jnp.float32)).astype(x.dtype)

def modulate(t, shift, scale):
    return t * (1 + scale) + shift

def swiglu(t, w_gu, w_down):
    gate, up = jnp.split(t @ w_gu, 2, axis=-1)
    return (jax.nn.silu(gate) * up) @ w_down

def axial_rope_tables(n_tokens, head_dim):
    rows = n_tokens // GRID_W
    row = jnp.broadcast_to(jnp.arange(rows)[:, None], (rows, GRID_W)).reshape(-1)
    col = jnp.broadcast_to(jnp.arange(GRID_W)[None, :], (rows, GRID_W)).reshape(-1)
    half = head_dim // 2
    inv = ROPE_BASE ** (-jnp.arange(0, half, 2, dtype=jnp.float32) / half)

    def axis_angles(pos):
        a = pos.astype(jnp.float32)[:, None] * inv[None, :]
        return jnp.concatenate([a, a], axis=-1)

    ang = jnp.concatenate([axis_angles(row), axis_angles(col)], axis=-1)
    return jnp.cos(ang), jnp.sin(ang)

def apply_axial_rope(x, cos, sin):
    q = x.shape[-1] // 4
    x32 = x.astype(jnp.float32)
    xr = x32.reshape(*x.shape[:-1], 2, 2, q)
    rot = jnp.stack([-xr[..., 1, :], xr[..., 0, :]], axis=-2).reshape(x.shape)
    return (x32 * cos + rot * sin).astype(x.dtype)

def sweep_query_blocks(fn, q):
    B, H, L, d = q.shape
    nb = L // Q_BLOCK_2
    qb = q.reshape(B, H, nb, Q_BLOCK_2, d).transpose(2, 0, 1, 3, 4)
    out = lax.map(fn, qb)
    return out.transpose(1, 2, 0, 3, 4).reshape(B, out.shape[2], L, out.shape[-1])

def diff_attention(h, hc, w_in, w_out, q_norm, k_norm, lq1, lk1, lq2, lk2, subln, lambda_init, ctx_out):
    f32 = jnp.float32
    L = h.shape[1]

    def project(t):
        Bt, Lt, _ = t.shape
        q, k, v = jnp.split(t @ w_in, 3, axis=-1)
        q = rmsnorm(q.reshape(Bt, Lt, 2 * DIFF_HEADS, DIFF_DH), q_norm).transpose(0, 2, 1, 3)
        k = rmsnorm(k.reshape(Bt, Lt, 2 * DIFF_HEADS, DIFF_DH), k_norm).transpose(0, 2, 1, 3)
        v = v.reshape(Bt, Lt, DIFF_HEADS, 2 * DIFF_DH).transpose(0, 2, 1, 3)
        return q, k, v

    q, k, v = project(h)
    qc, kc, vc = project(hc)
    cos, sin = axial_rope_tables(L, DIFF_DH)
    q = apply_axial_rope(q, cos, sin)
    k = apply_axial_rope(k, cos, sin)
    lam = (jnp.exp(jnp.sum(lq1.astype(f32) * lk1.astype(f32)))
           - jnp.exp(jnp.sum(lq2.astype(f32) * lk2.astype(f32))) + lambda_init)

    def pair(t):
        return t.reshape(t.shape[0], DIFF_HEADS, 2, t.shape[2], t.shape[3])

    def attend(qb, keys, vals):
        s = jnp.einsum('bhmtd,bhmsd->bhmts', pair(qb), keys).astype(f32) * DIFF_DH ** -0.5
        p = jax.nn.softmax(s, axis=-1)
        a = (p[:, :, 0] - lam * p[:, :, 1]).astype(vals.dtype)
        return jnp.einsum('bhts,bhse->bhte', a, vals)

    def finish(o):
        Bt, _, Lt, _ = o.shape
        o = rmsnorm(o, subln) * (1.0 - lambda_init)
        return o.transpose(0, 2, 1, 3).reshape(Bt, Lt, DIFF_HEADS * 2 * DIFF_DH) @ w_out

    keys = pair(jnp.concatenate([kc, k], axis=2))
    vals = jnp.concatenate([vc, v], axis=2)
    y = finish(sweep_query_blocks(lambda qb: attend(qb, keys, vals), q))
    yc = finish(attend(qc, pair(kc), vc)) if ctx_out else None
    return y, yc

def gqa_attention(h, hc, w_in, w_out, q_norm, k_norm, ctx_out):
    f32 = jnp.float32
    L = h.shape[1]
    kv_w = GQA_KV_HEADS * GQA_DH

    def project(t):
        Bt, Lt, _ = t.shape
        q, k, v = jnp.split(t @ w_in, [GQA_HEADS * GQA_DH, GQA_HEADS * GQA_DH + kv_w], axis=-1)
        q = rmsnorm(q.reshape(Bt, Lt, GQA_HEADS, GQA_DH), q_norm).transpose(0, 2, 1, 3)
        k = rmsnorm(k.reshape(Bt, Lt, GQA_KV_HEADS, GQA_DH), k_norm).transpose(0, 2, 1, 3)
        v = v.reshape(Bt, Lt, GQA_KV_HEADS, GQA_DH).transpose(0, 2, 1, 3)
        return q, k, v

    q, k, v = project(h)
    qc, kc, vc = project(hc)
    cos, sin = axial_rope_tables(L, GQA_DH)
    q = apply_axial_rope(q, cos, sin)
    k = apply_axial_rope(k, cos, sin)

    def attend(qb, keys, vals):
        Bq, _, T, _ = qb.shape
        qg = qb.reshape(Bq, GQA_KV_HEADS, GQA_GROUP, T, GQA_DH)
        s = jnp.einsum('bkgtd,bksd->bkgts', qg, keys).astype(f32) * GQA_DH ** -0.5
        p = jax.nn.softmax(s, axis=-1).astype(vals.dtype)
        o = jnp.einsum('bkgts,bksd->bkgtd', p, vals)
        return o.reshape(Bq, GQA_HEADS, T, GQA_DH)

    def finish(o):
        Bt, _, Lt, _ = o.shape
        return o.transpose(0, 2, 1, 3).reshape(Bt, Lt, GQA_HEADS * GQA_DH) @ w_out

    keys = jnp.concatenate([kc, k], axis=2)
    vals = jnp.concatenate([vc, v], axis=2)
    y = finish(sweep_query_blocks(lambda qb: attend(qb, keys, vals), q))
    yc = finish(attend(qc, kc, vc)) if ctx_out else None
    return y, yc

def gla_chunk_scan(q, k, v, g, s0):
    f32 = jnp.float32
    B, H, L, _ = q.shape
    n = L // GLA_CHUNK
    mask = jnp.tril(jnp.ones((GLA_CHUNK, GLA_CHUNK), dtype=bool))[:, :, None]

    def to_chunks(t):
        return t.reshape(B, H, n, GLA_CHUNK, t.shape[-1]).transpose(2, 0, 1, 3, 4)

    def step(S, inp):
        qc, kc, vc, gc = inp
        qf, kf, vf = qc.astype(f32), kc.astype(f32), vc.astype(f32)
        b = jnp.cumsum(gc.astype(f32), axis=-2)
        o_inter = jnp.einsum('bhtk,bhkv->bhtv', qf * jnp.exp(b), S)
        rel = jnp.where(mask, b[:, :, :, None, :] - b[:, :, None, :, :], -jnp.inf)
        A = jnp.einsum('bhtk,bhtsk,bhsk->bhts', qf, jnp.exp(rel), kf)
        o = o_inter + jnp.einsum('bhts,bhsv->bhtv', A, vf)
        b_last = b[:, :, -1, :]
        S = jnp.exp(b_last)[..., None] * S + jnp.einsum(
            'bhsk,bhsv->bhkv', kf * jnp.exp(b_last[:, :, None, :] - b), vf)
        return S, o.astype(v.dtype)

    S, o = lax.scan(step, s0, (to_chunks(q), to_chunks(k), to_chunks(v), to_chunks(g)))
    o = o.transpose(1, 2, 0, 3, 4).reshape(B, H, L, v.shape[-1])
    return o, S

def gla_mixer(h, hc, w_in, gw1_f, gw2_f, gb_f, gw1_b, gw2_b, gb_b, out_norm, w_out, ctx_out):
    B = h.shape[0]

    def project(t):
        Bt, Lt, _ = t.shape
        q, k, v, r = jnp.split(t @ w_in, [GLA_DK, 2 * GLA_DK, 2 * GLA_DK + GLA_DV], axis=-1)

        def heads(z, e):
            return z.reshape(Bt, Lt, GLA_HEADS, e).transpose(0, 2, 1, 3)

        def log_decay(w1, w2, b):
            return heads(jax.nn.log_sigmoid(((t @ w1) @ w2 + b).astype(jnp.float32)) / GLA_TAU, GLA_DK_H)

        return (heads(q, GLA_DK_H) * GLA_DK_H ** -0.5, heads(k, GLA_DK_H), heads(v, GLA_DV_H), r,
                log_decay(gw1_f, gw2_f, gb_f), log_decay(gw1_b, gw2_b, gb_b))

    def flip(z):
        return jnp.flip(z, axis=2)

    q, k, v, r, g_f, g_b = project(h)
    qc, kc, vc, rc, gc_f, gc_b = project(hc)
    zeros = jnp.zeros((B, GLA_HEADS, GLA_DK_H, GLA_DV_H), jnp.float32)
    oc_f, sc_f = gla_chunk_scan(qc, kc, vc, gc_f, zeros)
    oc_b, sc_b = gla_chunk_scan(flip(qc), flip(kc), flip(vc), flip(gc_b), zeros)
    o_f, _ = gla_chunk_scan(q, k, v, g_f, sc_f)
    o_b, _ = gla_chunk_scan(flip(q), flip(k), flip(v), flip(g_b), sc_b)

    def finish(o, gate_in):
        Bt, _, Lt, _ = o.shape
        o = rmsnorm(o, out_norm).transpose(0, 2, 1, 3).reshape(Bt, Lt, GLA_DV)
        return (o * jax.nn.silu(gate_in)) @ w_out

    y = finish(o_f + flip(o_b), r)
    yc = finish(oc_f + flip(oc_b), rc) if ctx_out else None
    return y, yc

def second_inputs(seed: int = 0) -> dict:
    key = jax.random.key(seed)
    ks = jax.random.split(key, 32)
    f32 = jnp.float32
    D = D_MODEL

    def nrm(k, shape, scale):
        return scale * jax.random.normal(k, shape, f32)

    def gain(k, shape):
        return 1.0 + 0.02 * jax.random.normal(k, shape, f32)

    return {
        'x': nrm(ks[0], (BATCH, SEQ, D), 1.0),
        'c': nrm(ks[1], (BATCH, D), 1.0),
        'ctx': nrm(ks[2], (BATCH, CTX_LEN, D), 1.0),
        'c_ctx': nrm(ks[3], (D,), 1.0),
        'ada_w': nrm(ks[4], (DEPTH, D, 6 * D), 0.5 * D ** -0.5),
        'ada_b': nrm(ks[5], (DEPTH, 6 * D), 0.01),
        'norm1_g': gain(ks[6], (DEPTH, D)),
        'norm2_g': gain(ks[7], (DEPTH, D)),
        'ffn_w_gu': nrm(ks[8], (DEPTH, D, 2 * FFN_HIDDEN), D ** -0.5),
        'ffn_w_down': nrm(ks[9], (DEPTH, FFN_HIDDEN, D), FFN_HIDDEN ** -0.5),
        'diff_w_in': nrm(ks[10], (N_A, D, 3 * D), D ** -0.5),
        'diff_w_out': nrm(ks[11], (N_A, D, D), D ** -0.5),
        'diff_q_norm': gain(ks[12], (N_A, DIFF_DH)),
        'diff_k_norm': gain(ks[13], (N_A, DIFF_DH)),
        'diff_lambda_q1': nrm(ks[14], (N_A, DIFF_DH), 0.1),
        'diff_lambda_k1': nrm(ks[15], (N_A, DIFF_DH), 0.1),
        'diff_lambda_q2': nrm(ks[16], (N_A, DIFF_DH), 0.1),
        'diff_lambda_k2': nrm(ks[17], (N_A, DIFF_DH), 0.1),
        'diff_subln': gain(ks[18], (N_A, 2 * DIFF_DH)),
        'gqa_w_in': nrm(ks[19], (N_B, D, GQA_HEADS * GQA_DH + 2 * GQA_KV_HEADS * GQA_DH), D ** -0.5),
        'gqa_w_out': nrm(ks[20], (N_B, GQA_HEADS * GQA_DH, D), (GQA_HEADS * GQA_DH) ** -0.5),
        'gqa_q_norm': gain(ks[21], (N_B, GQA_DH)),
        'gqa_k_norm': gain(ks[22], (N_B, GQA_DH)),
        'gla_w_in': nrm(ks[23], (N_C, D, 2 * GLA_DK + 2 * GLA_DV), D ** -0.5),
        'gla_gate_w1_fwd': nrm(ks[24], (N_C, D, GLA_GATE_RANK), D ** -0.5),
        'gla_gate_w2_fwd': nrm(ks[25], (N_C, GLA_GATE_RANK, GLA_DK), GLA_GATE_RANK ** -0.5),
        'gla_gate_b_fwd': nrm(ks[26], (N_C, GLA_DK), 0.01),
        'gla_gate_w1_bwd': nrm(ks[27], (N_C, D, GLA_GATE_RANK), D ** -0.5),
        'gla_gate_w2_bwd': nrm(ks[28], (N_C, GLA_GATE_RANK, GLA_DK), GLA_GATE_RANK ** -0.5),
        'gla_gate_b_bwd': nrm(ks[29], (N_C, GLA_DK), 0.01),
        'gla_out_norm': gain(ks[30], (N_C, GLA_DV_H)),
        'gla_w_out': nrm(ks[31], (N_C, GLA_DV, D), GLA_DV ** -0.5),
    }

def second_block(x, c, ctx, c_ctx, ada_w, ada_b, norm1_g, norm2_g, ffn_w_gu, ffn_w_down,
              diff_w_in, diff_w_out, diff_q_norm, diff_k_norm, diff_lambda_q1, diff_lambda_k1,
              diff_lambda_q2, diff_lambda_k2, diff_subln, gqa_w_in, gqa_w_out, gqa_q_norm, gqa_k_norm,
              gla_w_in, gla_gate_w1_fwd, gla_gate_w2_fwd, gla_gate_b_fwd, gla_gate_w1_bwd,
              gla_gate_w2_bwd, gla_gate_b_bwd, gla_out_norm, gla_w_out):
    xc = ctx
    cond_lat = jax.nn.silu(c)
    cond_ctx = jax.nn.silu(c_ctx)
    for i in range(DEPTH):
        last = i == DEPTH - 1
        mod = (cond_lat @ ada_w[i] + ada_b[i])[:, None, :]
        modc = (cond_ctx @ ada_w[i] + ada_b[i])[None, None, :]
        sh1, sc1, g1, sh2, sc2, g2 = jnp.split(mod, 6, axis=-1)
        csh1, csc1, cg1, csh2, csc2, cg2 = jnp.split(modc, 6, axis=-1)

        h = modulate(rmsnorm(x, norm1_g[i]), sh1, sc1)
        hc = modulate(rmsnorm(xc, norm1_g[i]), csh1, csc1)
        kind, j = i % N_MIXERS, i // N_MIXERS
        if kind == 0:
            lambda_init = 0.8 - 0.6 * math.exp(-0.3 * i)
            y, yc = diff_attention(h, hc, diff_w_in[j], diff_w_out[j], diff_q_norm[j], diff_k_norm[j],
                                   diff_lambda_q1[j], diff_lambda_k1[j], diff_lambda_q2[j],
                                   diff_lambda_k2[j], diff_subln[j], lambda_init, not last)
        elif kind == 1:
            y, yc = gqa_attention(h, hc, gqa_w_in[j], gqa_w_out[j], gqa_q_norm[j], gqa_k_norm[j], not last)
        else:
            y, yc = gla_mixer(h, hc, gla_w_in[j], gla_gate_w1_fwd[j], gla_gate_w2_fwd[j], gla_gate_b_fwd[j],
                              gla_gate_w1_bwd[j], gla_gate_w2_bwd[j], gla_gate_b_bwd[j],
                              gla_out_norm[j], gla_w_out[j], not last)

        x = x + g1 * y
        x = x + g2 * swiglu(modulate(rmsnorm(x, norm2_g[i]), sh2, sc2), ffn_w_gu[i], ffn_w_down[i])
        if not last:
            xc = xc + cg1 * yc
            xc = xc + cg2 * swiglu(modulate(rmsnorm(xc, norm2_g[i]), csh2, csc2), ffn_w_gu[i], ffn_w_down[i])
    return x


def setup_inputs(seed=0):
    out = dict(first_inputs(seed))
    for name, value in second_inputs(seed + 1).items():
        if name != "x":
            out[name + "_2"] = value
    return out


def reference(
    x, c, ada_w, ada_b, norm_g, ffn_w_in, ffn_w_out, a_w_in, a_conv, a_w_out, kv_norm_g,
    kv_ada_w, kv_ada_b, kv_w, cmp_pos, cmp_w1, cmp_w2, b_w_in, b_w_out, c_2, ctx_2, c_ctx_2,
    ada_w_2, ada_b_2, norm1_g_2, norm2_g_2, ffn_w_gu_2, ffn_w_down_2, diff_w_in_2, diff_w_out_2,
    diff_q_norm_2, diff_k_norm_2, diff_lambda_q1_2, diff_lambda_k1_2, diff_lambda_q2_2,
    diff_lambda_k2_2, diff_subln_2, gqa_w_in_2, gqa_w_out_2, gqa_q_norm_2, gqa_k_norm_2,
    gla_w_in_2, gla_gate_w1_fwd_2, gla_gate_w2_fwd_2, gla_gate_b_fwd_2, gla_gate_w1_bwd_2,
    gla_gate_w2_bwd_2, gla_gate_b_bwd_2, gla_out_norm_2, gla_w_out_2,
):
    x = first_block(
        x, c, ada_w, ada_b, norm_g, ffn_w_in, ffn_w_out, a_w_in, a_conv, a_w_out, kv_norm_g,
        kv_ada_w, kv_ada_b, kv_w, cmp_pos, cmp_w1, cmp_w2, b_w_in, b_w_out,
    )
    return second_block(
        x, c_2, ctx_2, c_ctx_2, ada_w_2, ada_b_2, norm1_g_2, norm2_g_2, ffn_w_gu_2,
        ffn_w_down_2, diff_w_in_2, diff_w_out_2, diff_q_norm_2, diff_k_norm_2, diff_lambda_q1_2,
        diff_lambda_k1_2, diff_lambda_q2_2, diff_lambda_k2_2, diff_subln_2, gqa_w_in_2,
        gqa_w_out_2, gqa_q_norm_2, gqa_k_norm_2, gla_w_in_2, gla_gate_w1_fwd_2,
        gla_gate_w2_fwd_2, gla_gate_b_fwd_2, gla_gate_w1_bwd_2, gla_gate_w2_bwd_2,
        gla_gate_b_bwd_2, gla_out_norm_2, gla_w_out_2,
    )


_drawn_inputs = setup_inputs


def setup_inputs(seed=0):
    import zlib

    import numpy as np

    out = dict(_drawn_inputs(seed))
    spreads = {}
    factors = {'ada_b': 2.814,
     'kv_norm_g': 3.07,
     'kv_ada_b': 8.0,
     'cmp_pos': 3.199,
     'ada_b_2': 5.0,
     'norm1_g_2': 8.0,
     'norm2_g_2': 8.0,
     'diff_q_norm_2': 8.0,
     'diff_k_norm_2': 8.0,
     'diff_lambda_q1_2': 64.0,
     'diff_lambda_k1_2': 64.0,
     'diff_lambda_q2_2': 8.0,
     'diff_lambda_k2_2': 8.0,
     'diff_subln_2': 8.0,
     'gqa_q_norm_2': 8.0,
     'gqa_k_norm_2': 8.0}
    for name, (base, spread) in spreads.items():
        noise = np.random.default_rng([zlib.crc32(name.encode()), seed]).standard_normal(out[name].shape)
        drawn = base * np.exp(spread * noise) if base else spread * noise
        out[name] = jnp.asarray(drawn.astype(out[name].dtype))
    for name, factor in factors.items():
        out[name] = (out[name] * factor).astype(out[name].dtype)
    return out
```

```python
from contextlib import ExitStack, contextmanager

import concourse.bass as bass
import numpy as np
from concourse import mybir

F32 = mybir.dt.float32
F32R = mybir.dt.float32r
ALU = mybir.AluOpType
ACT = mybir.ActivationFunctionType
AX_X = mybir.AxisListType.X

P = 128
D = 1024
KC = D // P
SEQ = 256
FF = 2816
FC = FF // P
UNIT = 2048
WCOL = UNIT // KC
RING = 3
ADA_RING = 2
EPS = 1e-6
DH = 64
HEADS = 16
GROUPS = 4
R = HEADS // GROUPS
CMP_LEN, CMP_STRIDE = 32, 16
N_CMP = (SEQ - CMP_LEN) // CMP_STRIDE + 1
NB = GROUPS * N_CMP
MASKED = -1e30
GELU_SCALE = (2.0 / np.pi) ** 0.5
GRID_W = 64
LAMBDA_INIT = 0.2
AHEAD = 2
VEC_UNITS = 4


class Tally:

    def __init__(self, marks=None):
        self.known = marks
        self.marks = {}
        self.now = {}

    def done(self, ins, sem, label=None, by=1):
        ins.then_inc(sem, by)
        self.now[sem.name] = self.now.get(sem.name, 0) + by
        if label is not None:
            assert label not in self.marks, label
            self.marks[label] = self.now[sem.name]

    def at(self, label):
        return 1 if self.known is None else self.known[label]


def trace(nc, t, io, out, stop):
    ctx = ExitStack()
    with ctx:
        def sb(name, shape, dt=F32):
            return ctx.enter_context(nc.sbuf_tensor(name, shape, dt))

        def sem(name):
            return ctx.enter_context(nc.semaphore(name))

        stage = sb("stage", [P, RING, UNIT])
        w_hi = sb("w_hi", [P, RING, UNIT], F32R)
        w_lo = sb("w_lo", [P, RING, UNIT], F32R)
        ada = sb("ada", [P, ADA_RING, UNIT])
        xs = sb("xs", [P, 4, D])
        h_hi = sb("h_hi", [P, KC * 512], F32R)
        h_lo = sb("h_lo", [P, KC * 512], F32R)
        mid = sb("mid", [P, FC * 512])
        silu_t = sb("silu_t", [P, 2, 512])
        gate_b = sb("gate_b", [P, 2, D])
        diag = sb("diag", [P, 2, 512])
        ident = sb("ident", [P, P])
        ones = sb("ones", [P, P])
        cols = sb("cols", [P, 512])
        modv = sb("modv", [P, 32, 16])
        modc = sb("modc", [P, 3, 16])
        ada_row = sb("ada_row", [P, 512])
        sel = sb("sel", [P, 4])
        cond = sb("cond", [P, 2, KC, 32])
        stat = sb("stat", [P, 32])
        w2 = sb("w2", [P, 4, DH])
        gsig = sb("gsig", [P, 2, 48])
        astat = sb("astat", [P, 2, 8, 4])
        bank = [ctx.enter_context(nc.psum_tensor(f"bank{i}", [P, 512], F32)) for i in range(8)]

        w_landed = [sem(f"w_landed{i}") for i in range(RING)]
        ada_landed = [sem(f"ada_landed{i}") for i in range(ADA_RING)]
        hi_done = sem("hi_done")
        lo_done = sem("lo_done")
        w_used = sem("w_used")
        ada_used = sem("ada_used")
        ada_rowed = sem("ada_rowed")
        ada_sum = sem("ada_sum")
        ada_col = sem("ada_col")
        part_done = [sem(f"part_done{i}") for i in range(3)]
        silu_done = sem("silu_done")
        mid_done = sem("mid_done")
        mhi_done = sem("mhi_done")
        mlo_done = sem("mlo_done")
        rows_landed = sem("rows_landed")
        x_landed = sem("x_landed")
        tables_landed = sem("tables_landed")
        lam_landed = sem("lam_landed")
        pe_s = sem("pe_s")
        dve_s = sem("dve_s")
        act_s = sem("act_s")
        pool_s = sem("pool_s")
        stored = sem("stored")

        col_at = {}
        pieces = []
        ncol = 0
        for name in ("ada_b", "kv_ada_b", "ada_b_2", "norm_g", "kv_norm_g", "norm1_g_2", "norm2_g_2",
                     "a_conv", "c", "c_2", "c_ctx_2", "cmp_pos", "diff_subln_2"):
            n = int(np.prod(io[name].shape)) // P
            flat = io[name]
            r = len(flat.shape)
            if name == "cmp_pos":
                flat = flat.rearrange("a (r l) d -> (a r) (l d)", l=P // DH)
            elif r == 1:
                flat = flat.rearrange("(r q) -> r q", q=P)
            elif r == 2:
                flat = flat.rearrange("a (r q) -> (a r) q", q=P)
            elif r == 3:
                flat = flat.rearrange("a b (r q) -> (a b r) q", q=P)
            else:
                flat = flat.rearrange("a b c (r q) -> (a b c r) q", q=P)
            col_at[name] = ncol
            pieces.append((ncol, n, flat))
            ncol += n
        assert ncol <= 512

        def rv(v):
            return v if v < 17 else v + 1

        def bias_col(v):
            if v < 9:
                return col_at["ada_b"] + v * KC
            if v < 11:
                return col_at["kv_ada_b"] + (v - 9) * KC
            if v < 20:
                return col_at["ada_b"] + (v - 2) * KC
            return col_at["ada_b_2"] + (v - 20) * KC

        def ada_src(v):
            if v < 9:
                return io["ada_w"][0], v
            if v < 11:
                return io["kv_ada_w"], v - 9
            if v < 20:
                return io["ada_w"][1], v - 11
            return io["ada_w_2"][(v - 20) // 6], (v - 20) % 6

        def norm_col(layer, sub, which):
            return col_at["norm_g"] + ((layer * 3 + sub) * 2 + which) * KC

        plan = [("prologue",)]
        N = dict(unit=0, vec=3, chunk=0, bstep=0, silu=0, step=[0, 0, 0])

        def add(kind, w_in, w_out, T, nvec, v0, g_pre, g_post, weight, steps, parts, bsteps, Td=None):
            s = dict(n=len(subs), kind=kind, Td=Td or T, w_in=w_in, w_out=w_out, T=T, v=N["vec"], nvec=nvec, v0=v0, u=N["unit"], c=N["chunk"],
                     b=N["bstep"], sc=N["silu"], sb=list(N["step"]), g_pre=g_pre, g_post=g_post, weight=weight,
                     post=g_post is not None, units=steps * parts, bsteps=bsteps)
            N["unit"] += steps * parts + bsteps
            N["vec"] += nvec
            N["chunk"] += 2 * steps if kind in ("ffn", "conv") else 0
            N["bstep"] += bsteps
            if kind == "ffn":
                N["silu"] += 2 * steps
            for q in range(parts if kind in ("ffn", "conv") else 0):
                N["step"][q] += steps
            subs.append(s)

        subs = []
        half, one = 0.5, 1.0
        add("ffn", io["ffn_w_in"][0, 0], io["ffn_w_out"][0, 0], 256, 5, 0, norm_col(0, 0, 0), norm_col(0, 0, 1), half, 11, 2, 11)
        add("conv", io["a_w_in"][0], io["a_w_out"][0], 256, 4, 3, norm_col(0, 1, 0), norm_col(0, 1, 1), one, 4, 3, 4)
        add("ffn", io["ffn_w_in"][0, 1], io["ffn_w_out"][0, 1], 256, 5, 6, norm_col(0, 2, 0), norm_col(0, 2, 1), half, 11, 2, 11)
        add("kv", io["kv_w"], None, 256, 0, 9, col_at["kv_norm_g"], None, one, 6, 1, 0)
        add("ffn", io["ffn_w_in"][1, 0], io["ffn_w_out"][1, 0], 256, 5, 11, norm_col(1, 0, 0), norm_col(1, 0, 1), half, 11, 2, 11)
        add("nsa", io["b_w_in"][0], io["b_w_out"][0], 256, 0, 14, norm_col(1, 1, 0), norm_col(1, 1, 1), one, 5, 1, 4)
        add("ffn", io["ffn_w_in"][1, 1], io["ffn_w_out"][1, 1], 256, 5, 17, norm_col(1, 2, 0), norm_col(1, 2, 1), half, 11, 2, 11)
        add("diff", io["diff_w_in_2"][0], io["diff_w_out_2"][0], 512, 0, 20, col_at["norm1_g_2"], None, one, 12, 1, 4)
        add("ffn", io["ffn_w_gu_2"][0], io["ffn_w_down_2"][0], 512, 5, 23, col_at["norm2_g_2"], None, one, 11, 2, 11)
        add("gqa", io["gqa_w_in_2"][0], io["gqa_w_out_2"][0], 512, 0, 26, col_at["norm1_g_2"] + KC, None, one, 6, 1, 4, Td=256)
        add("ffn", io["ffn_w_gu_2"][1], io["ffn_w_down_2"][1], 256, 0, 29, col_at["norm2_g_2"] + KC, None, one, 11, 2, 11)
        subs = subs[:stop]

        def x_mark(si, tt):
            prev = si - 1
            while prev >= 0 and (not subs[prev]["bsteps"] or tt >= subs[prev]["Td"] // P):
                prev -= 1
            return None if prev < 0 else (f"s{prev}", "x", tt)
        n_units = subs[-1]["u"] + subs[-1]["units"] + subs[-1]["bsteps"]

        def for_steps(eng, s, f):
            f(0, None)
            with eng.Fori(1, 3) as i:
                f(0, i)

        def for_b(eng, s, f):
            if s["bsteps"] == FC // 2:
                for j in range(RING):
                    f(j, None)
                with eng.Fori(1, 3) as i:
                    for j in range(RING):
                        f(j, i)
                for j in range(3 * RING, s["bsteps"]):
                    f(j, None)
            else:
                for j in range(s["bsteps"]):
                    f(j, None)

        def y_bank(T, tt, h):
            return bank[(4 + 2 * tt + h) % 8]

        def unit_part(s, tag, n, q):
            return (w_used, s["u"] + n + 1) if q else (pe_s, t.at((tag, "pu", n)))

        nsa_jobs = [(g, tt, br, N_CMP if br == 0 else (tt + 1) * P) for g in range(GROUPS) for tt in range(2) for br in (1, 2, 0)]

        flat_gate = gate_b[:, :, :].rearrange("p c d -> p (c d)")
        flat_diag = diag[:, :, :].rearrange("p h d -> p (h d)")
        flat_ada = ada[:, :, :].rearrange("p s n -> p (s n)")
        flat_astat = astat[:, :, :, :].rearrange("p b k r -> p (b k r)")

        class Wide:

            def __init__(w, s):
                w.diff = s["kind"] == "diff"
                w.dh = 64 if w.diff else 128
                w.hh = WCOL // w.dh
                w.rope = io["rope64"] if w.diff else io["rope128"]
                w.norms = ("diff_q_norm_2", "diff_k_norm_2") if w.diff else ("gqa_q_norm_2", "gqa_k_norm_2")
                w.nk = 8 if w.diff else 5
                if w.diff:
                    w.kT = mid[:, 0:4096].rearrange("p (c t) -> p c t", t=512)
                    w.v = mid[:, 4096:8192].rearrange("p (k c) -> p k c", k=4)
                    w.qT = flat_ada.rearrange("p (c t) -> p c t", t=512)
                else:
                    w.qT = mid[:, 2048:4096].rearrange("p (c t) -> p c t", t=256)
                    w.kT = mid[:, 4096:5120].rearrange("p (c t) -> p c t", t=512)
                    w.v = mid[:, 5120:6144].rearrange("p (k c) -> p k c", k=4)
                w.sq = mid[:, 10240:11264]

            def tiles(w, n):
                return 2 if not w.diff and n < 4 else 4

            def nat(w, n):
                return mid[:, 8192 + n % 2 * D:8192 + n % 2 * D + w.tiles(n) * WCOL]

            def dest(w, n, c):
                return w.qT[:, 2 * n + c, :] if n < 4 else w.kT[:, 2 * (n - 4) + c, :]

            def tables(w, n):
                k = 0 if n < 4 else 1
                return (flat_gate[:, k * 1024:k * 1024 + 512], flat_gate[:, k * 1024 + 512:k * 1024 + 1024],
                        flat_diag[:, 512 + k * 256:768 + k * 256])

        diff_jobs = [(h, tt, 0 if tt < 2 else 2) for h in range(8) for tt in range(4)]
        gqa_jobs = [(h, tt, 0) for h in range(8) for tt in range(2)]
        probs_d = [[mid[:, 8192 + b * D + m_ * 512:8192 + b * D + (m_ + 1) * 512] for m_ in range(2)] for b in range(2)]
        aT_d = [mid[:, 10240 + b * 512:10240 + (b + 1) * 512] for b in range(2)]
        probs_g = [mid[:, 6144 + b * 512:6144 + (b + 1) * 512] for b in range(2)]
        pT_g = [mid[:, 7168 + b * 512:7168 + (b + 1) * 512] for b in range(2)]
        lam_in = mid[:, 10240:10496].rearrange("p (k d) -> p k d", k=4)
        NEG_LAM = stat[:, 30:31]
        SUBLN = stat[:, 27:28]

        def wait_y(eng, s, tag, tt, h):
            if tt == s["Td"] // P - 1 and h == 1:
                eng.wait_ge(w_used, s["u"] + s["units"] + s["bsteps"])
            else:
                eng.wait_ge(pe_s, t.at((tag, "y", tt, h)))

        def xn(tt):
            return mid[:, tt * D:(tt + 1) * D]

        def sq(tt, T):
            o = (2 if T == 256 else 4) * D
            return mid[:, o + tt % 2 * D:o + (tt % 2 + 1) * D]

        def h32(idx, T):
            o = (4 if T == 256 else 6) * D + idx % 4 * 256
            return mid[:, o:o + 256]

        KEEP = FC * 256
        at = [KEEP]

        def keep(*shape):
            n = int(np.prod(shape))
            a = mid[:, at[0]:at[0] + n]
            at[0] += n
            return a

        kT = keep(2, GROUPS, 256).rearrange("p (b g t) -> p b g t", b=2, g=GROUPS)
        vn = keep(2, 2, 256).rearrange("p (b k c) -> p b k c", b=2, k=2)
        kcT = keep(NB)
        vc = keep(GROUPS * DH)
        dist = keep(2, 256).rearrange("p (t s) -> p t s", t=2)
        dist_c = keep(2, N_CMP).rearrange("p (t s) -> p t s", t=2)
        seen_c = keep(2, N_CMP).rearrange("p (t s) -> p t s", t=2)
        kc2 = mid[:, 0:2 * GROUPS * 272].rearrange("p (k g t) -> p k g t", k=2, g=GROUPS)
        blk = mid[:, 2176:2176 + 2 * 16 * NB].rearrange("p (k c n) -> p k c n", k=2, c=16)
        hx = silu_t[:, 0, 0:4 * NB].rearrange("p (h n) -> p h n", h=2)
        hx2 = silu_t[:, 0, 256:256 + 4 * NB].rearrange("p (h n) -> p h n", h=2)
        hx3 = silu_t[:, 1, 0:4 * NB].rearrange("p (h n) -> p h n", h=2)
        gT = silu_t[:, 1, 256:256 + 4 * NB].rearrange("p (h n) -> p h n", h=2)
        qT = mid[:, 2048:4096].rearrange("p (c t) -> p c t", c=KC)
        probs = [gate_b[:, i, :].rearrange("p (r s) -> p r s", r=R) for i in range(2)]
        pT = [mid[:, o:o + 1024].rearrange("p (k n) -> p k n", k=2) for o in (10240, 4096)]
        assert at[0] <= 9700
        conv_t = mid[:, 9700:9700 + 2 * 258].rearrange("p (q t) -> p q t", q=2)
        iota_t = mid[:, 10240:10496].bitcast(mybir.dt.int32)

        block = ctx.enter_context(nc.Block())

        @block.sync
        def _(sp):
            def load_unit(u, src, k, i=None, per=0, n=None):
                s = u % RING
                if u >= RING or i is not None:
                    sp.wait_ge(lo_done, u - RING + 1 + (0 if i is None else i * per))
                dst = stage[:, s, 0:k * (n or UNIT // k)].rearrange("p (k n) -> p k n", k=k)
                sp.dma_start(dst, src).then_inc(w_landed[s], 16)

            def load_vec(v, src, j, half, i=None):
                for q in (2 * half, 2 * half + 1):
                    n = rv(v) * VEC_UNITS + q
                    s = n % ADA_RING
                    if v == 27 and i is None:
                        sp.wait_ge(pe_s, t.at(("ada", "free")))
                    if n >= ADA_RING or i is not None:
                        sp.wait_ge(ada_used, n - ADA_RING + 1 + (0 if i is None else i * VEC_UNITS))
                    c0 = j * D if i is None else i * D + j * D
                    a = src[q * 2 * P:(q + 1) * 2 * P, bass.ds(c0, D)].rearrange("(k p) n -> p k n", p=P)
                    sp.dma_start(ada[:, s, :].rearrange("p (k n) -> p k n", k=2), a).then_inc(ada_landed[s], 16)

            def col_unit(w, c0):
                return w[:, bass.ds(c0, WCOL)].rearrange("(k p) n -> p k n", p=P)

            def row_unit(w, r0):
                return w[bass.ds(r0, 2 * P), :].rearrange("(k p) n -> p k n", p=P)

            n = 0
            for at, rows, flat in pieces:
                done = 0
                while done < rows:
                    k = min(rows - done, P - (at + done) % P)
                    r = (at + done) % P
                    c = (at + done) // P * P
                    sp.dma_start(diag[r:r + k, 0, c:c + P], flat[done:done + k, :]).then_inc(rows_landed, 16)
                    n += 16
                    done += k
            t.marks["small_rows"] = n
            sp.dma_start(w2[:, :, :], io["cmp_w2"].rearrange("k (h p) d -> p (k h) d", p=P)).then_inc(x_landed, 16)
            sp.dma_start(xs[:, 0:2, :], io["x"][0].rearrange("(t p) d -> p t d", p=P)).then_inc(x_landed, 16)
            sp.dma_start(xs[:, 2:4, :], io["ctx_2"][0].rearrange("(t p) d -> p t d", p=P)).then_inc(x_landed, 16)
            for v in range(3):
                load_vec(v, *ada_src(v), 0)
                load_vec(v, *ada_src(v), 1)

            def load_cmp(kv):
                for q in range(2):
                    n = 17 * VEC_UNITS + 2 * kv + q
                    sp.wait_ge(ada_used, n - ADA_RING + 1)
                    src = io["cmp_w1"][kv][q * D:(q + 1) * D, :].rearrange("(c p) h -> p c h", p=P)
                    sp.dma_start(ada[:, n % ADA_RING, :].rearrange("p (c h) -> p c h", c=KC), src).then_inc(ada_landed[n % ADA_RING], 16)

            cmp_late = []
            late = []

            def single_vec(v):
                for w in late:
                    load_vec(w, *ada_src(w), 1)
                late.clear()
                if v is not None:
                    load_vec(v, *ada_src(v), 0)
                    late.append(v)

            def b_units(s, u):
                def one_unit(j, i):
                    r0 = j * 2 * P if i is None else i * (RING * 2 * P) + j * 2 * P
                    load_unit(u + j, row_unit(s["w_out"], r0), 2, i, RING)
                    if j == 1 and i is None:
                        single_vec(None)
                for_b(sp, s, one_unit)

            for s in subs:
                u = s["u"]
                if s["kind"] == "ffn":
                    src, j0 = ada_src(s["v"]) if s["nvec"] else (None, 0)

                    def block3(k0, i):
                        for k in range(3):
                            c0 = k * WCOL if i is None else i * (3 * WCOL) + k * WCOL
                            c1 = FF + k * WCOL if i is None else i * (3 * WCOL) + (FF + k * WCOL)
                            load_unit(u + 2 * k, col_unit(s["w_in"], c0), KC, i, 6)
                            load_unit(u + 2 * k + 1, col_unit(s["w_in"], c1), KC, i, 6)
                            if i is None and cmp_late:
                                load_cmp(cmp_late.pop())
                            if k < 2 and s["nvec"]:
                                load_vec(s["v"], src, j0, k, i)
                    for_steps(sp, s, block3)
                    for k in (9, 10):
                        load_unit(u + 2 * k, col_unit(s["w_in"], k * WCOL), KC)
                        load_unit(u + 2 * k + 1, col_unit(s["w_in"], FF + k * WCOL), KC)
                        if s["nvec"]:
                            single_vec(s["v"] + k - 6)
                    b_units(s, u + 22)
                elif s["kind"] == "conv":
                    for k in range(4):
                        for part in (1, 2, 0):
                            load_unit(u, col_unit(s["w_in"], part * D + k * WCOL), KC)
                            u += 1
                        single_vec(s["v"] + k)
                    b_units(s, u)
                elif s["kind"] in ("kv", "nsa", "diff", "gqa"):
                    for k in range(s["units"]):
                        if s["kind"] == "nsa" and k == 4:
                            load_unit(u + k, s["w_in"][:, D:D + 48].rearrange("(k p) n -> p k n", p=P), KC, n=48)
                        else:
                            load_unit(u + k, col_unit(s["w_in"], k * WCOL), KC)
                    if s["kind"] == "kv":
                        load_cmp(0)
                        cmp_late.append(1)
                    else:
                        b_units(s, u + s["units"])
            sp.wait_ge(act_s, t.at("finished"))
            sp.dma_start(out[0].rearrange("(t p) d -> p t d", p=P), xs[:, 0:2, :]).then_inc(stored, 16)
            sp.wait_ge(stored, 16)

        @block.gpsimd
        def _(pool):
            g = nc.gpsimd
            g.memset(ones[:, :], 1.0)
            t.done(g.memset(cond[:, :, :, :], 0.0), pool_s, "ones")
            t.done(g.memset(ident[:, :], 0.0), pool_s, "id0")
            pool.wait_ge(pool_s, t.at("id0"))
            t.done(g.affine_select(out=ident[:, :], in_=ident[:, :], compare_op=ALU.not_equal, fill=1.0, base=0,
                                   pattern=[[-1, P]], channel_multiplier=1), pool_s, "ident")
            t.done(g.memset(sel[:, :], 0.0), pool_s, "sel0")
            pool.wait_ge(pool_s, t.at("sel0"))
            for j in range(4):
                for q in range(2):
                    last = g.affine_select(out=sel[:, j:j + 1], in_=sel[:, j:j + 1], compare_op=ALU.not_equal,
                                           fill=1.0, base=-(64 * q + 32 * (j % 2) + j // 2),
                                           pattern=[[0, 1]], channel_multiplier=1)
                    t.done(last, pool_s, ("sel", j, q))
                    pool.wait_ge(pool_s, t.at(("sel", j, q)))

            for tt in range(2):
                t.done(g.iota(iota_t[:, 0:256], pattern=[[1, 256]], base=-tt * P, channel_multiplier=-1), pool_s, ("iota", tt))
                pool.wait_ge(pool_s, t.at(("iota", tt)))
                t.done(g.tensor_copy(dist[:, tt, :], iota_t[:, 0:256]), pool_s, ("dist0", tt))
                pool.wait_ge(pool_s, t.at(("dist0", tt)))
                t.done(g.affine_select(out=dist[:, tt, :], in_=dist[:, tt, :], compare_op=ALU.is_ge, fill=MASKED,
                                       base=tt * P, pattern=[[-1, 256]], channel_multiplier=1), pool_s, ("dist", tt))
                first_end = CMP_LEN - 1 - tt * P
                t.done(g.iota(iota_t[:, 0:N_CMP], pattern=[[CMP_STRIDE, N_CMP]], base=first_end, channel_multiplier=-1), pool_s, ("iotac", tt))
                t.done(g.memset(seen_c[:, tt, :], 1.0), pool_s, ("seen0", tt))
                pool.wait_ge(pool_s, t.at(("seen0", tt)))
                t.done(g.tensor_copy(dist_c[:, tt, :], iota_t[:, 0:N_CMP]), pool_s, ("distc0", tt))
                pool.wait_ge(pool_s, t.at(("distc0", tt)))
                for buf, fill in ((dist_c, MASKED), (seen_c, 0.0)):
                    last = g.affine_select(out=buf[:, tt, :], in_=buf[:, tt, :], compare_op=ALU.is_ge, fill=fill,
                                           base=-first_end, pattern=[[-CMP_STRIDE, N_CMP]], channel_multiplier=1)
                t.done(last, pool_s, ("distances", tt))
                pool.wait_ge(pool_s, t.at(("distances", tt)))

            for s in subs:
                if s["kind"] in ("diff", "gqa"):
                    w = Wide(s)
                    pool.wait_ge(dve_s, t.at(x_mark(s["n"], 1)))
                    for k in range(2):
                        g.dma_start(flat_diag[:, k * 256:k * 256 + 2 * w.dh].rearrange("p (t d) -> p t d", t=2),
                                    w.rope[k].rearrange("(t p) d -> p t d", p=P)).then_inc(tables_landed, 16)
                    for k in range(2):
                        src = io[w.norms[k]][0].partition_broadcast(P).unsqueeze(1).broadcast_to([P, w.hh, w.dh])
                        g.dma_start(flat_diag[:, 512 + k * 256:768 + k * 256].rearrange("p (h d) -> p h d", d=w.dh),
                                    src).then_inc(tables_landed, 16)
                    if w.diff:
                        for k, name in enumerate(("q1", "k1", "q2", "k2")):
                            g.dma_start(lam_in[:, k, :], io[f"diff_lambda_{name}_2"][0].partition_broadcast(P)).then_inc(lam_landed, 16)

        @block.scalar
        def _(act):
            a = nc.scalar

            def split(n, i=None, per=0):
                if i is None and n >= n_units:
                    return
                s = n % RING
                k = 0 if i is None else i * per
                act.wait_ge(w_landed[s], 16 * (n // RING + 1) + (0 if i is None else i * (16 * per // RING)))
                if n >= RING or i is not None:
                    act.wait_ge(w_used, n - RING + 1 + k)
                a.copy(w_hi[:, s, :], stage[:, s, :]).then_inc(hi_done, 1)

            def mid_split(s, j, i=None, first=False):
                T = s["Td"]
                o = 0 if s["T"] == 512 else KC * 256
                slot = j % RING
                c = 2 * j * T if i is None else i * (2 * RING * T) + 2 * j * T
                k = 0 if i is None else i * RING
                u = s["u"] + s["units"] + j
                if s["T"] == 512 and j == 0 and i is None:
                    act.wait_ge(w_used, u)
                elif j >= RING or i is not None:
                    act.wait_ge(w_used, u - RING + 1 + k)
                if s["kind"] not in ("ffn", "conv"):
                    act.wait_ge(act_s, t.at((f"s{s['n']}", "o")))
                elif i is None:
                    act.wait_ge(mid_done, s["c"] + (2 * j + 2 if j < RING else 2 * s["bsteps"]))
                a.copy(h_hi[:, o + slot * 2 * T:o + (slot + 1) * 2 * T], mid[:, bass.ds(c, 2 * T)]).then_inc(mhi_done, 1)

            def norm_root(tt, tag):
                act.wait_ge(dve_s, t.at((tag, "mean", tt)))
                t.done(a.activation(stat[:, 8 + tt:9 + tt], stat[:, 4 + tt:5 + tt], ACT.Sqrt), act_s, (tag, "root", tt))

            def stream_stats(s, tt):
                tag = f"s{s['n']}"
                mark = x_mark(s["n"], tt)
                if mark is None:
                    act.wait_ge(x_landed, 48)
                else:
                    act.wait_ge(dve_s, t.at(mark))
                if tt >= 2:
                    act.wait_ge(act_s, t.at((tag, "ss", tt - 2)))
                t.done(a.activation(sq(tt, s["T"]), xs[:, tt, :], ACT.Square, accum_out=stat[:, tt:tt + 1]), act_s, (tag, "ss", tt))
                norm_root(tt, tag)

            def stream_norm(s, tt):
                tag = f"s{s['n']}"
                act.wait_ge(dve_s, t.at((tag, "rstd", tt)))
                t.done(a.activation(xn(tt), xs[:, tt, :], ACT.Copy, scale=stat[:, 12 + tt:13 + tt]), act_s, (tag, "xn", tt))

            def product_stats(s, tt):
                tag = f"s{s['n']}"
                if s["post"]:
                    for h in range(2):
                        wait_y(act, s, tag, tt, h)
                        t.done(a.activation(sq(tt, s["Td"])[:, h * 512:(h + 1) * 512], y_bank(s["Td"], tt, h)[:, :], ACT.Square,
                                            accum_out=stat[:, 16 + 2 * tt + h:17 + 2 * tt + h]), act_s, (tag, "ss", tt, h))
                    norm_root(tt, tag + "y")

            def between(prev, s):
                n_prev = prev["Td"] // P if prev and prev["bsteps"] else 0
                for tt in range(n_prev):
                    product_stats(prev, tt)
                    if tt and s:
                        stream_stats(s, tt - 1)
                        stream_norm(s, tt - 1)
                for tt in range(max(n_prev - 1, 0), s["T"] // P if s else 0):
                    stream_stats(s, tt)
                    stream_norm(s, tt)

            tables_used = []

            def table(func):
                n = len(tables_used)
                tables_used.append(func)
                if n:
                    act.wait_ge(act_s, t.at(("table", n - 1)))
                else:
                    act.wait_ge(pool_s, t.at("ident"))
                t.done(a.activation(stat[:, 26:27], ident[:, 0:1], func), act_s, ("table", n))

            def prep(s, tag):
                T = s["T"]
                for k in range(KC):
                    for c in range(T // 256):
                        act.wait_ge(dve_s, t.at((tag, "h32", k, c)))
                        o = k * T + c * 256
                        t.done(a.copy(h_hi[:, o:o + 256], h32(k * (T // 256) + c, T)), act_s, (tag, "hi", k, c))

            def gates(s, tag):
                for c in range(s["Td"] // 256):
                    for h in range(2):
                        act.wait_ge(pe_s, t.at((tag, "gate", c, h)))
                        t.done(a.copy(gate_b[:, c, h * 512:(h + 1) * 512], bank[6 + h][:, :]), act_s, (tag, "gateb", c, h))

            def kv_act(s, tag):
                u = s["u"]
                for n in range(6):
                    split(u + n + AHEAD)
                    if n in (2, 4):
                        for q in range(2):
                            act.wait_ge(*unit_part(s, tag, n, q))
                            for src in range(2):
                                for dst in range(2):
                                    ins = a.copy(kT[64 * dst:64 * dst + 64, n // 2 - 1, 2 * q + src, :],
                                                 bank[2 * (n % 2) + q][64 * src:64 * src + 64, 0:256])
                            t.done(ins, act_s, (tag, "ev", n, q))
                    elif n in (3, 5):
                        act.wait_ge(w_used, u + n + 1)
                        t.done(a.copy(vn[:, n // 2 - 1, :, :], bank[2 * (n % 2)][:, :].rearrange("p (k c) -> p k c", k=2)), act_s, (tag, "ev", n, 0))
                act.wait_ge(dve_s, t.at((tag, "gin")))
                t.done(a.activation(hx2, hx3, ACT.Tanh, scale=GELU_SCALE), act_s, (tag, "tanh"))
                act.wait_ge(pe_s, t.at((tag, "kc")))
                a.mul(kcT[0:64, :], bank[6][0:64, 0:NB], 0.5)
                a.mul(kcT[64:128, :], bank[7][64:128, 0:NB], 0.5)
                t.done(a.mul(vc[0:N_CMP, :], bank[5][0:N_CMP, 0:GROUPS * DH], 0.5), act_s, (tag, "kept"))

            def nsa_act(s, tag):
                u = s["u"]
                for n in range(4):
                    split(u + n + AHEAD)
                    for q in range(2):
                        act.wait_ge(*unit_part(s, tag, n, q))
                        t.done(a.mul(qT[:, 2 * n + q, :], bank[2 * (n % 2) + q][:, 0:256], DH ** -0.5), act_s, (tag, "ev", n, q))
                split(u + 4 + AHEAD)
                act.wait_ge(w_used, u + 5)
                t.done(a.activation(gsig[:, :, :], bank[0][:, 0:96].rearrange("p (t c) -> p t c", t=2), ACT.Exp, scale=-1.0), act_s, (tag, "gexp"))
                jobs = nsa_jobs
                for J in range(len(jobs) + 3):
                    if J < len(jobs):
                        g, tt, br, nk = jobs[J]
                        act.wait_ge(dve_s, t.at((tag, "neg", J)))
                        for r in range(R):
                            ins = a.activation(probs[J % 2][:, r, 0:nk], probs[J % 2][:, r, 0:nk], ACT.Exp,
                                               bias=astat[:, J % 2, 1, r:r + 1], accum_out=astat[:, J % 2, 2, r:r + 1])
                        t.done(ins, act_s, (tag, "exp", J))
                    if 0 <= J - 2 < len(jobs):
                        i = J - 2
                        g, tt, br, nk = jobs[i]
                        act.wait_ge(pe_s, t.at((tag, "jt", i)))
                        if br == 0:
                            ins = a.copy(pT[i % 2][0:N_CMP, 0, :], bank[4][0:N_CMP, :])
                        else:
                            for kt in range(tt + 1):
                                ins = a.copy(pT[i % 2][:, kt, :], bank[4 + kt][:, :])
                        t.done(ins, act_s, (tag, "evT", i))
                    if 0 <= J - 3 and jobs[J - 3][2] == 0:
                        g, tt, br, nk = jobs[J - 3]
                        act.wait_ge(pe_s, t.at((tag, "pv", J - 3)))
                        b = bank[6 + ((J - 3) // 3) % 2][0:64, :].rearrange("p (c r q) -> p c r q", c=2, r=2)
                        o = mid[:, 0:2048].rearrange("p (c t) -> p c t", c=KC)[:, 2 * g:2 * g + 2, tt * P:(tt + 1) * P]
                        a.copy(o[0:64], b[:, :, 0, :])
                        t.done(a.copy(o[64:128], b[:, :, 1, :]), act_s, (tag, "evO", J - 3))
                t.marks[(tag, "o")] = t.now["act_s"]

            def wide_act(s, tag):
                w, u = Wide(s), s["u"]
                if w.diff:
                    act.wait_ge(dve_s, t.at((tag, "lsum")))
                    t.done(a.activation(stat[:, 28:30], stat[:, 28:30], ACT.Exp), act_s, (tag, "lexp"))
                for n in range(s["units"] + 1):
                    if n < s["units"]:
                        split(u + n + AHEAD)
                        nt = w.tiles(n)
                        for half in range(nt // 2):
                            act.wait_ge(*unit_part(s, tag, n, half or nt == 2))
                            b = bank[2 * (n % 2) + half][:, :]
                            if n < w.nk:
                                if 2 <= n:
                                    act.wait_ge(pe_s, t.at((tag, "ut", n - 2)))
                                dst = w.nat(n)[:, half * 512:(half + 1) * 512]
                            else:
                                c0 = (n - w.nk) * WCOL
                                dst = w.v[:, 2 * half:2 * half + 2, c0:c0 + WCOL]
                                b = b.rearrange("p (k c) -> p k c", k=2)
                            t.done(a.copy(dst, b), act_s, (tag, "ev", n, half))
                        if n < w.nk:
                            if n:
                                act.wait_ge(dve_s, t.at((tag, "rsum", n - 1)))
                            act.wait_ge(act_s, t.at((tag, "ev", n, nt // 2 - 1)))
                            t.done(a.activation(w.sq[:, 0:nt * WCOL], w.nat(n), ACT.Square), act_s, (tag, "sq", n))
                            act.wait_ge(dve_s, t.at((tag, "rmean", n)))
                            k = nt * w.hh
                            t.done(a.activation(flat_astat[:, 32:32 + k], flat_astat[:, 16:16 + k], ACT.Sqrt), act_s, (tag, "rroot", n))
                    i = n - 1
                    if 0 <= i < w.nk:
                        act.wait_ge(pe_s, t.at((tag, "ut", i)))
                        for c in range(2):
                            k = w.tiles(i) * P
                            if w.diff and i == 0 and c == 0:
                                act.wait_ge(ada_used, (rv(26) + 1) * VEC_UNITS)
                            ins = a.copy(w.dest(i, c), bank[4 + c][:, 0:k])
                        t.done(ins, act_s, (tag, "evu", i))
                if w.diff:
                    diff_act(s, tag, w)
                else:
                    gqa_act(s, tag, w)

            def diff_act(s, tag, w):
                jobs = diff_jobs
                for J in range(len(jobs) + 3):
                    if J < len(jobs):
                        h, tt, k0 = jobs[J]
                        b, nk = J % 2, (4 - k0) * P
                        act.wait_ge(dve_s, t.at((tag, "neg", J)))
                        if J >= 2:
                            act.wait_ge(pe_s, t.at((tag, "jt", J - 2)))
                        for m_ in range(2):
                            ins = a.activation(probs_d[b][m_][:, 0:nk], bank[2 * b + m_][:, 0:nk], ACT.Exp,
                                               bias=astat[:, b, 1, m_:m_ + 1], accum_out=astat[:, b, 2, m_:m_ + 1])
                        t.done(ins, act_s, (tag, "exp", J))
                    if 0 <= J - 2 < len(jobs):
                        i = J - 2
                        nk = (4 - jobs[i][2]) * P
                        act.wait_ge(pe_s, t.at((tag, "jt", i)))
                        t.done(a.copy(aT_d[i % 2][:, 0:nk], bank[4 + i % 2][:, 0:nk]), act_s, (tag, "evT", i))
                    if 0 <= J - 3 and jobs[J - 3][1] == 3:
                        h = jobs[J - 3][0]
                        act.wait_ge(pe_s, t.at((tag, "pv", J - 3)))
                        t.done(a.copy(w.qT[:, h, :], bank[6 + h % 2][:, :]), act_s, (tag, "evO", h))
                        act.wait_ge(act_s, t.at((tag, "evO", h)))
                        if h >= 2:
                            act.wait_ge(dve_s, t.at((tag, "osum", h - 2)))
                        t.done(a.activation(silu_t[:, h % 2, :], w.qT[:, h, :], ACT.Square), act_s, (tag, "osq", h))
                act.wait_ge(dve_s, t.at((tag, "omean")))
                t.done(a.activation(ada_row[:, 64:96], ada_row[:, 32:64], ACT.Sqrt), act_s, (tag, "oroot"))
                for h in range(8):
                    act.wait_ge(pe_s, t.at((tag, "ot", h)))
                    t.done(a.activation(mid[:, h * 512:(h + 1) * 512], bank[h % 4][:, :], ACT.Copy, scale=SUBLN), act_s, (tag, "evo", h))
                t.marks[(tag, "o")] = t.now["act_s"]

            def gqa_act(s, tag, w):
                jobs = gqa_jobs
                for J in range(len(jobs) + 3):
                    if J < len(jobs):
                        b = J % 2
                        act.wait_ge(dve_s, t.at((tag, "neg", J)))
                        if J >= 2:
                            act.wait_ge(pe_s, t.at((tag, "jt", J - 2)))
                        t.done(a.activation(probs_g[b], bank[b][:, :], ACT.Exp, bias=astat[:, b, 1, 0:1],
                                            accum_out=astat[:, b, 2, 0:1]), act_s, (tag, "exp", J))
                    if 0 <= J - 2 < len(jobs):
                        i = J - 2
                        act.wait_ge(pe_s, t.at((tag, "jt", i)))
                        t.done(a.copy(pT_g[i % 2], bank[2 + i % 2][:, :]), act_s, (tag, "evT", i))
                    if 0 <= J - 3 and jobs[J - 3][1] == 1:
                        h = jobs[J - 3][0]
                        act.wait_ge(pe_s, t.at((tag, "pv", J - 3)))
                        t.done(a.copy(mid[:, h * 256:(h + 1) * 256], bank[4 + h % 2][:, 0:256]), act_s, (tag, "evO", h))
                t.marks[(tag, "o")] = t.now["act_s"]

            act.wait_ge(dve_s, t.at("cols"))
            act.wait_ge(pool_s, t.at("ones"))
            for b, name in enumerate(("c", "c_2")):
                a.activation(cond[:, b, :, 0], cols[:, col_at[name]:col_at[name] + KC], ACT.Silu)
            t.done(a.activation(cond[:, 1, :, 1], cols[:, col_at["c_ctx_2"]:col_at["c_ctx_2"] + KC], ACT.Silu), act_s, "cond")
            split(0)
            split(1)
            act.wait_ge(x_landed, 48)
            for si, s in enumerate(subs):
                tag = f"s{si}"
                if si and subs[si - 1]["bsteps"]:
                    table(ACT.Sqrt)
                between(subs[si - 1] if si else None, s)
                if s["kind"] == "ffn":
                    table(ACT.Silu)
                prep(s, tag)
                u, c = s["u"], s["c"]
                T = s["T"]
                if s["kind"] == "ffn":
                    def step(j, i=None):
                        per = 6
                        split(u + 2 * j + 2, i, per)
                        ci = 0 if i is None else i * 6
                        for q in range(2):
                            if q == 0:
                                act.wait_ge(part_done[0], s["sb"][0] + j + 1 + (0 if i is None else i * 3))
                            else:
                                act.wait_ge(w_used, u + 2 * j + 1 + ci)
                            if c + 2 * j + q >= 2 or i is not None:
                                act.wait_ge(mid_done, c + 2 * j + q - 1 + ci)
                            a.activation(silu_t[:, q, 0:T], bank[q][:, 0:T], ACT.Silu).then_inc(silu_done, 1)
                        split(u + 2 * j + 3, i, per)

                    for_steps(act, s, lambda j0, i: [step(j, i) for j in range(3)])
                    step(9)
                    if T == 256:
                        mid_split(s, 0)
                    step(10)
                elif s["kind"] == "conv":
                    for j in range(4):
                        for q in range(3):
                            split(u + 3 * j + q + 2)
                    mid_split(s, 0)
                elif s["kind"] == "kv":
                    kv_act(s, tag)
                    continue
                elif s["kind"] == "nsa":
                    nsa_act(s, tag)
                elif s["kind"] in ("diff", "gqa"):
                    wide_act(s, tag)
                gates(s, tag)
                if s["kind"] not in ("ffn", "conv") or T == 512:
                    mid_split(s, 0)
                for_b(act, s, lambda j, i: (split(s["u"] + s["units"] + j + AHEAD, i, RING),
                                            mid_split(s, j + 1, i) if (i is not None or j + 1 < s["bsteps"]) else None))
            between(subs[-1], None)
            act.wait_ge(dve_s, t.at(x_mark(len(subs), 1)))
            t.done(a.copy(stat[:, 31:32], stat[:, 8:9]), act_s, "finished")

        @block.vector
        def _(dve):
            v = nc.vector

            def split(n, i=None, per=0):
                if i is None and n >= n_units:
                    return
                s = n % RING
                dve.wait_ge(hi_done, n + 1 + (0 if i is None else i * per))
                v.tensor_tensor(w_lo[:, s, :], stage[:, s, :], w_hi[:, s, :].bitcast(F32), ALU.subtract).then_inc(lo_done, 1)

            def mid_split(s, j, i=None):
                T = s["Td"]
                o = 0 if s["T"] == 512 else KC * 256
                slot = j % RING
                c = 2 * j * T if i is None else i * (2 * RING * T) + 2 * j * T
                r = slice(o + slot * 2 * T, o + (slot + 1) * 2 * T)
                dve.wait_ge(mhi_done, s["b"] + j + 1 + (0 if i is None else i * RING))
                v.tensor_tensor(h_lo[:, r], mid[:, bass.ds(c, 2 * T)], h_hi[:, r].bitcast(F32), ALU.subtract).then_inc(mlo_done, 1)

            def vec_row(vi, i=None):
                dve.wait_ge(ada_used, (rv(vi) + 1) * VEC_UNITS + (0 if i is None else i * VEC_UNITS))
                v.tensor_copy(ada_row[:, :], bank[4][:, :]).then_inc(ada_rowed, 1)

            def vec_col(vi, i=None):
                dve.wait_ge(ada_sum, rv(vi) + 1 + (0 if i is None else i))
                src = bank[5][:, 0:16].rearrange("p (c s h) -> p s h c", c=4, s=2)
                for st in range(2):
                    if i is None:
                        dst, b = modv[:, vi, 8 * st:8 * st + 8], cols[:, bias_col(vi):bias_col(vi) + 8]
                    else:
                        flat = modv[:, :, :].rearrange("p v c -> p (v c)")
                        dst = flat[:, bass.ds(i * 16 + (vi * 16 + 8 * st), 8)]
                        b = cols[:, bass.ds(i * 8 + bias_col(vi), 8)]
                    ins = v.tensor_tensor(dst.rearrange("p (h c) -> p h c", h=2), src[:, st], b.rearrange("p (h c) -> p h c", h=2), ALU.add)
                ins.then_inc(ada_col, 1)

            def norm_mean(tt, tag):
                t.done(v.tensor_scalar(stat[:, 4 + tt:5 + tt], stat[:, tt:tt + 1], 1.0 / D, EPS, ALU.mult, ALU.add), dve_s, (tag, "mean", tt))
                dve.wait_ge(act_s, t.at((tag, "root", tt)))
                t.done(v.reciprocal(stat[:, 12 + tt:13 + tt], stat[:, 8 + tt:9 + tt]), dve_s, (tag, "rstd", tt))

            def stream_norm(s, tt):
                tag = f"s{s['n']}"
                dve.wait_ge(act_s, t.at((tag, "ss", tt)))
                norm_mean(tt, tag)

            def between(prev, s):
                n_prev = prev["Td"] // P if prev and prev["bsteps"] else 0
                for tt in range(n_prev):
                    finish(prev, tt, (lambda: stream_norm(s, tt - 1)) if tt and s else None)
                for tt in range(max(n_prev - 1, 0), s["T"] // P if s else 0):
                    stream_norm(s, tt)

            def mod_in(s, tag):
                dve.wait_ge(ada_col, rv(s["v0"] + 1) + 1)
                for st in range(s["T"] // 256):
                    g = cols[:, s["g_pre"]:s["g_pre"] + 8]
                    t.done(v.scalar_tensor_tensor(out=modc[:, 0, 8 * st:8 * st + 8], in0=modv[:, s["v0"] + 1, 8 * st:8 * st + 8],
                                                  scalar=1.0, in1=g, op0=ALU.add, op1=ALU.mult), dve_s, (tag, "A", st))

            def prep(s, tag):
                T = s["T"]
                n = T // 256
                for k in range(KC):
                    for c in range(n):
                        b = bank[4 + (k * T // 512) % 4]
                        o = (k * T) % 512 + c * 256
                        dve.wait_ge(pe_s, t.at((tag, "tr", k * T // 512)))
                        idx = k * n + c
                        if idx >= 4:
                            dve.wait_ge(dve_s, t.at((tag, "lo", (idx - 4) // n, (idx - 4) % n)))
                        t.done(v.tensor_scalar(h32(idx, T), b[:, o:o + 256], modc[:, 0, 8 * c + k:8 * c + k + 1],
                                               modv[:, s["v0"], 8 * c + k:8 * c + k + 1], ALU.mult, ALU.add), dve_s, (tag, "h32", k, c))
                        if idx >= 1:
                            lo(tag, T, n, idx - 1)
                lo(tag, T, n, KC * n - 1)

            def lo(tag, T, n, idx):
                k, c = idx // n, idx % n
                dve.wait_ge(act_s, t.at((tag, "hi", k, c)))
                o = k * T + c * 256
                t.done(v.tensor_tensor(h_lo[:, o:o + 256], h32(idx, T), h_hi[:, o:o + 256].bitcast(F32), ALU.subtract),
                       dve_s, (tag, "lo", k, c))

            def gates(s, tag):
                dve.wait_ge(ada_col, rv(s["v0"] + 2) + 1)
                for st in range(s["Td"] // 256):
                    gv = modv[:, s["v0"] + 2, 8 * st:8 * st + 8]
                    if s["post"]:
                        t.done(v.scalar_tensor_tensor(out=modc[:, 2, 8 * st:8 * st + 8], in0=gv, scalar=s["weight"],
                                                      in1=cols[:, s["g_post"]:s["g_post"] + 8], op0=ALU.mult, op1=ALU.mult), dve_s, (tag, "G", st))
                        gv = modc[:, 2, 8 * st:8 * st + 8]
                        dve.wait_ge(dve_s, t.at((tag, "G", st)))
                    for h in range(2):
                        if st:
                            dve.wait_ge(pe_s, t.at((tag, "gate", st - 1, h)))
                        for k in range(4):
                            ins = v.tensor_scalar(diag[:, h, k * P:(k + 1) * P], ident[:, :], gv[:, 4 * h + k:4 * h + k + 1], None, ALU.mult)
                        t.done(ins, dve_s, (tag, "diag", st, h))

            def finish(s, tt, previous_norm):
                tag, T = f"s{s['n']}", s["Td"]
                if s["post"]:
                    dve.wait_ge(act_s, t.at((tag, "ss", tt, 1)))
                    t.done(v.tensor_tensor(stat[:, tt:tt + 1], stat[:, 16 + 2 * tt:17 + 2 * tt], stat[:, 17 + 2 * tt:18 + 2 * tt], ALU.add),
                           dve_s, (tag, "ssum", tt))
                    dve.wait_ge(dve_s, t.at((tag, "ssum", tt)))
                    norm_mean(tt, tag + "y")
                    dve.wait_ge(dve_s, t.at((tag + "y", "rstd", tt)))
                dve.wait_ge(act_s, t.at((tag, "gateb", T // 256 - 1, 1)))
                for h in range(2):
                    wait_y(dve, s, tag, tt, h)
                    o = xn(tt)[:, h * 512:(h + 1) * 512]
                    g = gate_b[:, tt // 2, h * 512:(h + 1) * 512]
                    if s["post"]:
                        t.done(v.scalar_tensor_tensor(out=o, in0=y_bank(T, tt, h)[:, :], scalar=stat[:, 12 + tt:13 + tt], in1=g,
                                                      op0=ALU.mult, op1=ALU.mult), dve_s, (tag, "upd", tt, h))
                    else:
                        t.done(v.tensor_tensor(o, y_bank(T, tt, h)[:, :], g, ALU.mult), dve_s, (tag, "upd", tt, h))
                if previous_norm:
                    previous_norm()
                dve.wait_ge(dve_s, t.at((tag, "upd", tt, 1)))
                t.done(v.tensor_tensor(xs[:, tt, :], xs[:, tt, :], xn(tt), ALU.add), dve_s, (tag, "x", tt))

            def kv_dve(s, tag):
                u = s["u"]
                for n in range(6):
                    split(u + n + AHEAD)
                    if n < 2:
                        for q in range(2):
                            dve.wait_ge(*unit_part(s, tag, n, q))
                            for src in range(2):
                                b = bank[2 * (n % 2) + q][64 * src:64 * src + 64, 0:256]
                                v.tensor_copy(kc2[0:64, n, 2 * q + src, 0:256], b)
                                ins = v.tensor_copy(kc2[64:128, n, 2 * q + src, 0:255], b[:, 1:256])
                            t.done(ins, dve_s, (tag, "ev", n, q))
                for kv in range(2):
                    for c in range(16):
                        dve.wait_ge(dve_s, t.at((tag, "ev", kv, 1)))
                        src = kc2[:, kv, :, 2 * c:2 * c + CMP_STRIDE * (N_CMP - 1) + 1:CMP_STRIDE]
                        col = col_at["cmp_pos"] + kv * 16 + c
                        ins = v.tensor_scalar(blk[:, kv, c, :].rearrange("p (g n) -> p g n", g=GROUPS), src,
                                              cols[:, col:col + 1], None, ALU.add)
                    t.done(ins, dve_s, (tag, "blk", kv))
                dve.wait_ge(ada_sum, 18)
                v.tensor_copy(hx[:, 0, :], bank[4][:, 0:2 * NB])
                v.tensor_copy(hx[:, 1, :], bank[5][:, 0:2 * NB]).then_inc(ada_rowed, 1)
                dve.wait_ge(ada_rowed, 18)
                t.done(v.tensor_tensor(hx2, hx, hx, ALU.mult), dve_s, (tag, "sq"))
                dve.wait_ge(dve_s, t.at((tag, "sq")))
                t.done(v.tensor_scalar(hx3, hx2, 0.044715, 1.0, ALU.mult, ALU.add), dve_s, (tag, "poly"))
                dve.wait_ge(dve_s, t.at((tag, "poly")))
                t.done(v.tensor_tensor(hx3, hx3, hx, ALU.mult), dve_s, (tag, "gin"))
                dve.wait_ge(act_s, t.at((tag, "tanh")))
                v.scalar_tensor_tensor(out=gT, in0=hx2, scalar=1.0, in1=hx, op0=ALU.add, op1=ALU.mult).then_inc(ada_col, 1)

            def nsa_dve(s, tag):
                u = s["u"]
                for n in range(5):
                    split(u + n + AHEAD)
                dve.wait_ge(pool_s, t.at(("distances", 1)))
                dve.wait_ge(act_s, t.at((tag, "gexp")))
                t.done(v.tensor_scalar(gsig[:, :, :], gsig[:, :, :], 1.0, None, ALU.add), dve_s, (tag, "g1"))
                dve.wait_ge(dve_s, t.at((tag, "g1")))
                t.done(v.reciprocal(gsig[:, :, :], gsig[:, :, :]), dve_s, (tag, "gsig"))
                jobs = nsa_jobs
                for J in range(len(jobs) + 1):
                    if J < len(jobs):
                        g, tt, br, nk = jobs[J]
                        b = J % 2
                        d = dist_c[:, tt, :] if br == 0 else dist[:, tt, 0:nk]
                        dve.wait_ge(pe_s, t.at((tag, "s", J)))
                        if J >= 2:
                            dve.wait_ge(pe_s, t.at((tag, "jt", J - 2)))
                        for r in range(R):
                            slope = 2.0 ** (-8.0 * (g * R + r + 1) / HEADS)
                            sc = bank[2 * b + r % 2][:, r // 2 * 256:r // 2 * 256 + nk]
                            ins = v.scalar_tensor_tensor(out=probs[b][:, r, 0:nk], in0=d, scalar=slope, in1=sc, op0=ALU.mult, op1=ALU.add)
                        t.done(ins, dve_s, (tag, "bias", J))
                        dve.wait_ge(dve_s, t.at((tag, "bias", J)))
                        t.done(v.reduce_max(astat[:, b, 0, :], probs[b][:, :, 0:nk], AX_X), dve_s, (tag, "max", J))
                        dve.wait_ge(dve_s, t.at((tag, "max", J)))
                        t.done(v.tensor_scalar(astat[:, b, 1, :], astat[:, b, 0, :], -1.0, None, ALU.mult), dve_s, (tag, "neg", J))
                    if 0 <= J - 1:
                        i = J - 1
                        b = i % 2
                        g, tt, br, nk = jobs[i]
                        dve.wait_ge(act_s, t.at((tag, "exp", i)))
                        den = astat[:, b, 2, :]
                        pr = probs[b][:, :, 0:nk]
                        if br == 0:
                            m = seen_c[:, tt, :].unsqueeze(1).broadcast_to([P, R, nk])
                            t.done(v.tensor_tensor(pr, pr, m, ALU.mult), dve_s, (tag, "mask", i))
                            dve.wait_ge(dve_s, t.at((tag, "mask", i)))
                            t.done(v.reduce_sum(den, pr, AX_X), dve_s, (tag, "den", i))
                            dve.wait_ge(dve_s, t.at((tag, "den", i)))
                        t.done(v.tensor_scalar(astat[:, b, 3, :], den, 1e-30, None, ALU.max), dve_s, (tag, "dmax", i))
                        dve.wait_ge(dve_s, t.at((tag, "dmax", i)))
                        t.done(v.reciprocal(astat[:, b, 4, :], astat[:, b, 3, :]), dve_s, (tag, "inv", i))
                        dve.wait_ge(dve_s, t.at((tag, "inv", i)))
                        gate = gsig[:, tt, br * HEADS + g * R:br * HEADS + (g + 1) * R]
                        t.done(v.tensor_tensor(astat[:, b, 5, :], astat[:, b, 4, :], gate, ALU.mult), dve_s, (tag, "coef", i))
                        dve.wait_ge(dve_s, t.at((tag, "coef", i)))
                        cf = astat[:, b, 5, :].unsqueeze(2).broadcast_to([P, R, nk])
                        t.done(v.tensor_tensor(pr, pr, cf, ALU.mult), dve_s, (tag, "p", i))

            def wide_dve(s, tag):
                w, u = Wide(s), s["u"]
                dh, hh = w.dh, w.hh
                q4 = dh // 4
                dve.wait_ge(tables_landed, 64 if w.diff or subs[0]["kind"] == "gqa" else 128)
                if w.diff:
                    dve.wait_ge(lam_landed, 64)
                    t.done(v.tensor_tensor(lam_in[:, 0:4:2, :], lam_in[:, 0:4:2, :], lam_in[:, 1:4:2, :], ALU.mult), dve_s, (tag, "lmul"))
                    dve.wait_ge(dve_s, t.at((tag, "lmul")))
                    t.done(v.reduce_sum(stat[:, 28:30], lam_in[:, 0:4:2, :], AX_X), dve_s, (tag, "lsum"))
                    dve.wait_ge(act_s, t.at((tag, "lexp")))
                    t.done(v.scalar_tensor_tensor(out=NEG_LAM, in0=stat[:, 29:30], scalar=-LAMBDA_INIT, in1=stat[:, 28:29],
                                                  op0=ALU.add, op1=ALU.subtract), dve_s, (tag, "lam"))
                    c = col_at["diff_subln_2"]
                    v.tensor_scalar(SUBLN, cols[:, c:c + 1], 1.0 - LAMBDA_INIT, None, ALU.mult)
                v.tensor_scalar(flat_diag[:, 512:768], flat_diag[:, 512:768], float(dh) ** -0.5, None, ALU.mult)
                neg = flat_diag[:, 256:256 + 2 * dh].rearrange("p (x a q) -> p x a q", a=2, q=q4)[:, :, 0]
                t.done(v.tensor_scalar(neg, neg, -1.0, None, ALU.mult), dve_s, (tag, "tneg"))
                dve.wait_ge(dve_s, t.at((tag, "tneg")))
                for k in range(2):
                    cg, sg, gain = w.tables(4 * k)
                    for tt in range(2):
                        cos = flat_diag[:, tt * dh:(tt + 1) * dh].unsqueeze(1).broadcast_to([P, hh, dh])
                        v.tensor_tensor(cg[:, tt * 256:(tt + 1) * 256].rearrange("p (h d) -> p h d", h=hh), cos,
                                        gain.rearrange("p (h d) -> p h d", h=hh), ALU.mult)
                        for h in range(hh):
                            for part in range(2):
                                o = tt * 256 + h * dh
                                out_ = sg[:, o:o + dh].rearrange("p (a b q) -> p a b q", a=2, b=2)[:, :, part]
                                sin = flat_diag[:, 256 + tt * dh:256 + (tt + 1) * dh].rearrange("p (a b q) -> p a b q", a=2, b=2)[:, :, part]
                                gg = gain[:, 0:dh].rearrange("p (a b q) -> p a b q", a=2, b=2)[:, :, 1 - part]
                                ins = v.tensor_tensor(out_, sin, gg, ALU.mult)
                t.done(ins, dve_s, (tag, "tables"))
                for n in range(s["units"]):
                    split(u + n + AHEAD)
                    if n < w.nk:
                        nt = w.tiles(n)
                        k = nt * hh
                        nat = w.nat(n)
                        cg, sg, gain = w.tables(n)
                        dve.wait_ge(act_s, t.at((tag, "sq", n)))
                        t.done(v.reduce_sum(flat_astat[:, 0:k], w.sq[:, 0:nt * WCOL].rearrange("p (n d) -> p n d", d=dh), AX_X), dve_s, (tag, "rsum", n))
                        dve.wait_ge(dve_s, t.at((tag, "rsum", n)))
                        t.done(v.tensor_scalar(flat_astat[:, 16:16 + k], flat_astat[:, 0:k], 1.0 / dh, EPS, ALU.mult, ALU.add), dve_s, (tag, "rmean", n))
                        dve.wait_ge(act_s, t.at((tag, "rroot", n)))
                        t.done(v.reciprocal(flat_astat[:, 48:48 + k], flat_astat[:, 32:32 + k]), dve_s, (tag, "rinv", n))
                        dve.wait_ge(dve_s, t.at((tag, "rinv", n)))
                        rs = flat_astat[:, 48:48 + k].unsqueeze(2).broadcast_to([P, k, dh])
                        n3 = nat.rearrange("p (n d) -> p n d", d=dh)
                        t.done(v.tensor_tensor(n3, n3, rs, ALU.mult), dve_s, (tag, "rn", n))
                        dve.wait_ge(dve_s, t.at((tag, "rn", n)))
                        if nt == 4:
                            c3 = nat[:, 512:1024].rearrange("p (t c) -> p t c", t=2)
                            v.tensor_tensor(c3, c3, gain.unsqueeze(1).broadcast_to([P, 2, WCOL]), ALU.mult)
                        t1, t2, x = silu_t[:, 0, :], silu_t[:, 1, :], nat[:, 0:512]
                        pair = lambda z, j: z.rearrange("p (x b q) -> p x b q", b=2, q=q4)[:, :, j]
                        v.tensor_tensor(t1, x, cg, ALU.mult)
                        v.tensor_tensor(pair(t2, 0), pair(x, 1), pair(sg, 0), ALU.mult)
                        t.done(v.tensor_tensor(pair(t2, 1), pair(x, 0), pair(sg, 1), ALU.mult), dve_s, (tag, "rot", n))
                        dve.wait_ge(dve_s, t.at((tag, "rot", n)))
                        t.done(v.tensor_tensor(x, t1, t2, ALU.add), dve_s, (tag, "rope", n))
                if w.diff:
                    diff_dve(s, tag, w)
                else:
                    gqa_dve(s, tag, w)

            def diff_dve(s, tag, w):
                jobs = diff_jobs
                def osum(h):
                    dve.wait_ge(act_s, t.at((tag, "osq", h)))
                    t.done(v.reduce_sum(ada_row[:, 4 * h:4 * h + 4], silu_t[:, h % 2, :].rearrange("p (t d) -> p t d", t=4), AX_X), dve_s, (tag, "osum", h))
                for J in range(len(jobs) + 1):
                    if J < len(jobs):
                        h, tt, k0 = jobs[J]
                        b, nk = J % 2, (4 - k0) * P
                        dve.wait_ge(pe_s, t.at((tag, "s", J)))
                        for m_ in range(2):
                            ins = v.reduce_max(astat[:, b, 0, m_:m_ + 1], bank[2 * b + m_][:, 0:nk], AX_X)
                        t.done(ins, dve_s, (tag, "max", J))
                        dve.wait_ge(dve_s, t.at((tag, "max", J)))
                        t.done(v.tensor_scalar(astat[:, b, 1, 0:2], astat[:, b, 0, 0:2], -1.0, None, ALU.mult), dve_s, (tag, "neg", J))
                    if 0 <= J - 1:
                        i = J - 1
                        b, nk = i % 2, (4 - jobs[i][2]) * P
                        p0, p1 = probs_d[b][0][:, 0:nk], probs_d[b][1][:, 0:nk]
                        dve.wait_ge(act_s, t.at((tag, "exp", i)))
                        t.done(v.reciprocal(astat[:, b, 3, 0:2], astat[:, b, 2, 0:2]), dve_s, (tag, "inv", i))
                        dve.wait_ge(dve_s, t.at((tag, "inv", i)))
                        t.done(v.tensor_scalar(astat[:, b, 4, 0:1], astat[:, b, 3, 1:2], NEG_LAM, None, ALU.mult), dve_s, (tag, "coef", i))
                        t.done(v.tensor_scalar(p0, p0, astat[:, b, 3, 0:1], None, ALU.mult), dve_s, (tag, "p0", i))
                        dve.wait_ge(dve_s, t.at((tag, "p0", i)))
                        t.done(v.scalar_tensor_tensor(out=p0, in0=p1, scalar=astat[:, b, 4, 0:1], in1=p0, op0=ALU.mult, op1=ALU.add), dve_s, (tag, "p", i))
                    if J >= 8 and J % 4 == 0:
                        osum((J - 8) // 4)
                osum(7)
                dve.wait_ge(dve_s, t.at((tag, "osum", 7)))
                t.done(v.tensor_scalar(ada_row[:, 32:64], ada_row[:, 0:32], 1.0 / P, EPS, ALU.mult, ALU.add), dve_s, (tag, "omean"))
                dve.wait_ge(act_s, t.at((tag, "oroot")))
                t.done(v.reciprocal(ada_row[:, 96:128], ada_row[:, 64:96]), dve_s, (tag, "oinv"))
                dve.wait_ge(dve_s, t.at((tag, "oinv")))
                for h in range(8):
                    o = w.qT[:, h, :].rearrange("p (t d) -> p t d", t=4)
                    rs = ada_row[:, 96 + 4 * h:100 + 4 * h].unsqueeze(2).broadcast_to([P, 4, P])
                    t.done(v.tensor_tensor(o, o, rs, ALU.mult), dve_s, (tag, "on", h))

            def gqa_dve(s, tag, w):
                jobs = gqa_jobs
                for J in range(len(jobs) + 1):
                    if J < len(jobs):
                        b = J % 2
                        dve.wait_ge(pe_s, t.at((tag, "s", J)))
                        t.done(v.reduce_max(astat[:, b, 0, 0:1], bank[b][:, :], AX_X), dve_s, (tag, "max", J))
                        dve.wait_ge(dve_s, t.at((tag, "max", J)))
                        t.done(v.tensor_scalar(astat[:, b, 1, 0:1], astat[:, b, 0, 0:1], -1.0, None, ALU.mult), dve_s, (tag, "neg", J))
                    if 0 <= J - 1:
                        i = J - 1
                        b = i % 2
                        dve.wait_ge(act_s, t.at((tag, "exp", i)))
                        t.done(v.reciprocal(astat[:, b, 3, 0:1], astat[:, b, 2, 0:1]), dve_s, (tag, "inv", i))
                        dve.wait_ge(dve_s, t.at((tag, "inv", i)))
                        t.done(v.tensor_scalar(probs_g[b], probs_g[b], astat[:, b, 3, 0:1], None, ALU.mult), dve_s, (tag, "p", i))

            dve.wait_ge(pe_s, t.at("cols_t"))
            t.done(v.tensor_copy(cols[:, 0:ncol], bank[0][:, 0:ncol]), dve_s, "cols")
            for vi in range(3):
                vec_row(vi)
                vec_col(vi)
            split(0)
            split(1)
            for si, s in enumerate(subs):
                tag = f"s{si}"
                mod_in(s, tag)
                between(subs[si - 1] if si else None, s)
                prep(s, tag)
                u, c, T = s["u"], s["c"], s["T"]
                if s["kind"] == "ffn":
                    def step(j, i=None):
                        split(u + 2 * j + 2, i, 6)
                        split(u + 2 * j + 3, i, 6)
                        for q in range(2):
                            k = 0 if i is None else i * 6
                            dve.wait_ge(silu_done, s["sc"] + 2 * j + q + 1 + k)
                            if q == 0:
                                dve.wait_ge(part_done[1], s["sb"][1] + j + 1 + (0 if i is None else i * 3))
                            else:
                                dve.wait_ge(w_used, u + 2 * j + 2 + k)
                            o = (2 * j + q) * T if i is None else i * (6 * T) + (2 * j + q) * T
                            v.tensor_tensor(mid[:, bass.ds(o, T)], silu_t[:, q, 0:T], bank[2 + q][:, 0:T], ALU.mult).then_inc(mid_done, 1)

                    def block3(j0, i):
                        for j in range(3):
                            step(j, i)
                            if j == 1 and s["nvec"]:
                                vec_row(s["v"], i)
                        if s["nvec"]:
                            vec_col(s["v"], i)
                    for_steps(dve, s, block3)
                    for j in (9, 10):
                        if j == 10 and T == 256:
                            gates(s, tag)
                            mid_split(s, 0)
                        step(j)
                        if s["nvec"]:
                            vec_row(s["v"] + j - 6)
                            vec_col(s["v"] + j - 6)
                    if T == 512:
                        gates(s, tag)
                elif s["kind"] == "conv":
                    w0 = col_at["a_conv"]
                    for j in range(4):
                        split(u + 3 * j + 2)
                        split(u + 3 * j + 3)
                        split(u + 3 * j + 4)
                        if j == 3:
                            gates(s, tag)
                        for q in range(2):
                            n = c + 2 * j + q
                            k = 2 * j + q
                            cs, vp = silu_t[:, q, 0:256], conv_t[:, q, 0:258]
                            y1, y2 = silu_t[:, q, 256:512], silu_t[:, q, 0:256]
                            L = lambda x: (tag, x, k)
                            if k >= 2:
                                dve.wait_ge(mid_done, n - 1)
                            t.done(v.memset(vp[:, 0:2], 0.0), dve_s, L("z"))
                            if q == 0:
                                dve.wait_ge(part_done[1], s["sb"][1] + j + 1)
                            else:
                                dve.wait_ge(w_used, u + 3 * j + 2)
                            t.done(v.tensor_copy(cs, bank[q][:, 0:256]), dve_s, L("c"))
                            dve.wait_ge(dve_s, t.at(L("c")))
                            t.done(v.tensor_tensor(vp[:, 2:258], cs, bank[2 + q][:, 0:256], ALU.mult), dve_s, L("v"))
                            dve.wait_ge(dve_s, t.at(L("v")))
                            w = lambda m: cols[:, w0 + m * KC + k:w0 + m * KC + k + 1]
                            t.done(v.tensor_scalar(y1, vp[:, 0:256], w(0), None, ALU.mult), dve_s, L("y0"))
                            dve.wait_ge(dve_s, t.at(L("y0")))
                            t.done(v.scalar_tensor_tensor(out=y2, in0=vp[:, 1:257], scalar=w(1), in1=y1, op0=ALU.mult, op1=ALU.add), dve_s, L("y1"))
                            dve.wait_ge(dve_s, t.at(L("y1")))
                            t.done(v.scalar_tensor_tensor(out=y1, in0=vp[:, 2:258], scalar=w(2), in1=y2, op0=ALU.mult, op1=ALU.add), dve_s, L("y2"))
                            dve.wait_ge(dve_s, t.at(L("y2")))
                            if q == 0:
                                dve.wait_ge(part_done[2], s["sb"][2] + j + 1)
                            else:
                                dve.wait_ge(w_used, u + 3 * j + 3)
                            v.tensor_tensor(mid[:, k * T:(k + 1) * T], y1, bank[6 + q][:, 0:256], ALU.mult).then_inc(mid_done, 1)
                        vec_row(s["v"] + j)
                        vec_col(s["v"] + j)
                    mid_split(s, 0)
                elif s["kind"] == "kv":
                    kv_dve(s, tag)
                    continue
                elif s["kind"] == "nsa":
                    nsa_dve(s, tag)
                    gates(s, tag)
                elif s["kind"] in ("diff", "gqa"):
                    wide_dve(s, tag)
                    gates(s, tag)
                if s["kind"] not in ("ffn", "conv") or T == 512:
                    mid_split(s, 0)
                for_b(dve, s, lambda j, i: (split(s["u"] + s["units"] + j + AHEAD, i, RING),
                                            mid_split(s, j + 1, i) if (i is not None or j + 1 < s["bsteps"]) else None))
            between(subs[-1], None)

        @block.tensor
        def _(pe):
            m = nc.tensor

            def vec_acc(vi, half, i=None):
                b = 0 if vi < 20 else 1
                for q in (2 * half, 2 * half + 1):
                    n = rv(vi) * VEC_UNITS + q
                    s = n % ADA_RING
                    pe.wait_ge(ada_landed[s], 16 * (n // ADA_RING + 1) + (0 if i is None else i * (16 * VEC_UNITS // ADA_RING)))
                    for k in range(2):
                        for h in range(2):
                            z = 32 * (2 * k + h)
                            ins = m.matmul(bank[4][z:z + 32, :], cond[:, b, 2 * q + k, :],
                                           ada[:, s, k * D + h * 512:k * D + (h + 1) * 512],
                                           start=(q == 0), stop=(q == VEC_UNITS - 1), tile_position=(0, z))
                    ins.then_inc(ada_used, 1)

            def vec_sum(vi, i=None):
                k = 0 if i is None else i
                if vi or i is not None:
                    pe.wait_ge(ada_col, rv(vi) + k)
                pe.wait_ge(ada_rowed, rv(vi) + 1 + k)
                for c in range(4):
                    ins = m.matmul(bank[5][:, 4 * c:4 * c + 4], ada_row[:, c * P:(c + 1) * P], sel[:, :], start=True, stop=True)
                ins.then_inc(ada_sum, 1)

            def cols_product(dst, slot, q, T, tag=None):
                for k in range(KC):
                    if tag is not None:
                        pe.wait_ge(dve_s, t.at((tag, "lo", k, T // 256 - 1)))
                    wh = w_hi[:, slot, k * WCOL + q * P:k * WCOL + (q + 1) * P]
                    wl = w_lo[:, slot, k * WCOL + q * P:k * WCOL + (q + 1) * P]
                    m.matmul(dst[:, 0:T], wh, h_hi[:, k * T:(k + 1) * T], start=(k == 0), stop=False)
                    m.matmul(dst[:, 0:T], wh, h_lo[:, k * T:(k + 1) * T], start=False, stop=False)
                    ins = m.matmul(dst[:, 0:T], wl, h_hi[:, k * T:(k + 1) * T], start=False, stop=(k == KC - 1))
                return ins

            def prep(s, tag):
                T = s["T"]
                for g in range(KC * T // 512):
                    if g >= 4:
                        pe.wait_ge(dve_s, t.at((tag, "h32", g - 4, 1)))
                    for q in range(512 // P):
                        tt = q % (T // P)
                        k = g * 512 // T + q // (T // P)
                        if g == 0:
                            pe.wait_ge(act_s, t.at((tag, "xn", tt)))
                        ins = m.transpose(bank[4 + g % 4][:, q * P:(q + 1) * P], xn(tt)[:, k * P:(k + 1) * P], ident[:, :])
                    t.done(ins, pe_s, (tag, "tr", g))
                g = 4 * (T // 256 - 1)
                pe.wait_ge(dve_s, t.at((tag, "h32", (g + 1) * 512 // T - 1, T // 256 - 1)))

            def gates(s, tag):
                for c in range(s["Td"] // 256):
                    for h in range(2):
                        if c:
                            pe.wait_ge(act_s, t.at((tag, "gateb", c - 1, h)))
                        pe.wait_ge(dve_s, t.at((tag, "diag", c, h)))
                        t.done(m.matmul(bank[6 + h][:, :], ones[:, :], diag[:, h, :], start=True, stop=True), pe_s, (tag, "gate", c, h))

            def down(s, tag, vec):
                T = s["Td"]
                o = 0 if s["T"] == 512 else KC * 256
                u = s["u"] + s["units"]
                if vec is None:
                    pe.wait_ge(ada_col, rv(s["v"] + s["nvec"] - 1) + 1)
                pe.wait_ge(act_s, t.at((tag, "gateb", T // 256 - 1, 1)))
                if T == 512 and s["kind"] == "ffn":
                    pe.wait_ge(mid_done, s["c"] + 2 * s["bsteps"])

                def step(j, i):
                    if j == s["bsteps"] - 1:
                        for tt in range(T // P):
                            products(j, None, (tt,))
                    elif j == 0 and i is None and vec is not None:
                        products(j, i, (1,), (0,), 0)
                        vec_acc(vec, 1)
                        products(j, i, (1,), (1,), 0)
                        vec_sum(vec)
                        pe.wait_ge(ada_col, rv(vec) + 1)
                        products(j, i, (0,), end_tile=0)
                    else:
                        products(j, i, range(T // P))

                def products(j, i, tiles, kcs=(0, 1), end_tile=T // P - 1):
                    slot, ms = (u + j) % RING, j % RING
                    k = 0 if i is None else i * RING
                    pe.wait_ge(lo_done, u + j + 1 + k)
                    pe.wait_ge(mlo_done, s["b"] + j + 1 + k)
                    for kc in kcs:
                        first = i is None and j == 0 and kc == 0
                        last = j == s["bsteps"] - 1 and kc == 1
                        for tt in tiles:
                            r = o + (2 * ms + kc) * T + tt * P
                            passes = ((h_hi, w_hi), (h_hi, w_lo), (h_lo, w_hi))
                            for n, (a_, w_) in enumerate(passes):
                                for h in range(2):
                                    ins = m.matmul(y_bank(T, tt, h)[:, :], a_[:, r:r + P],
                                                   w_[:, slot, kc * D + h * 512:kc * D + (h + 1) * 512],
                                                   start=first and n == 0, stop=last and n == 2)
                                    end = kc == 1 and tt == end_tile and n == 2 and h == 1
                                    if end:
                                        ins.then_inc(w_used, 1)
                                    elif last and n == 2:
                                        t.done(ins, pe_s, (tag, "y", tt, h))

                for_b(pe, s, step)

            def rows_product(s, tag, dst, slot, tt, width, first):
                T = s["T"]
                for k in range(KC):
                    if first:
                        pe.wait_ge(dve_s, t.at((tag, "lo", k, T // 256 - 1)))
                    r = slice(k * T + tt * P, k * T + (tt + 1) * P)
                    c = slice(k * width, (k + 1) * width)
                    m.matmul(dst, h_hi[:, r], w_hi[:, slot, c], start=(k == 0), stop=False)
                    m.matmul(dst, h_hi[:, r], w_lo[:, slot, c], start=False, stop=False)
                    ins = m.matmul(dst, h_lo[:, r], w_hi[:, slot, c], start=False, stop=(k == KC - 1))
                return ins

            def kv_pe(s, tag):
                u, T = s["u"], s["T"]
                for n in range(6):
                    pe.wait_ge(lo_done, u + n + 1)
                    for q in range(2):
                        if n >= 2 and not (n in (3, 5) and q):
                            eng, who = (dve_s, n - 2) if n < 4 else (act_s, n - 2)
                            if (n - 2) % 2 == 0 or n - 2 == 1 or q == 0:
                                pe.wait_ge(eng, t.at((tag, "ev", who, q)))
                        if n in (3, 5):
                            ins = rows_product(s, tag, bank[2 * (n % 2)][:, q * 256:(q + 1) * 256], (u + n) % RING, q, WCOL, False)
                            if q:
                                ins.then_inc(w_used, 1)
                        else:
                            ins = cols_product(bank[2 * (n % 2) + q], (u + n) % RING, q, T, tag if n == 0 and q == 0 else None)
                            if q:
                                ins.then_inc(w_used, 1)
                            else:
                                t.done(ins, pe_s, (tag, "pu", n))
                for q in range(VEC_UNITS):
                    n = 17 * VEC_UNITS + q
                    kv = q // 2
                    pe.wait_ge(ada_landed[n % ADA_RING], 16 * (n // ADA_RING + 1))
                    pe.wait_ge(dve_s, t.at((tag, "blk", kv)))
                    for c in range(KC):
                        for hc in range(2):
                            ins = m.matmul(bank[4 + hc][:, kv * NB:(kv + 1) * NB],
                                           ada[:, n % ADA_RING, c * 256 + hc * P:c * 256 + (hc + 1) * P],
                                           blk[:, kv, q % 2 * KC + c, :], start=(q % 2 == 0 and c == 0), stop=(q % 2 == 1 and c == KC - 1))
                    ins.then_inc(ada_used, 1)
                m.matmul(bank[6][0:64, 0:64], ones[:, 0:64], ones[:, 0:64], start=True, stop=True).then_inc(ada_sum, 1)
                pe.wait_ge(ada_col, 18)
                for half in range(2):
                    for hc in range(2):
                        m.matmul(bank[6 + half][64 * half:64 * half + 64, 0:NB], w2[:, hc, :], gT[:, hc, 0:NB],
                                 start=(hc == 0), stop=(hc == 1), tile_position=(0, 64 * half))
                for g in range(GROUPS):
                    for hc in range(2):
                        ins = m.matmul(bank[5][0:N_CMP, g * DH:(g + 1) * DH], gT[:, hc, NB + g * N_CMP:NB + (g + 1) * N_CMP],
                                       w2[:, 2 + hc, :], start=(hc == 0), stop=(hc == 1))
                t.done(ins, pe_s, (tag, "kc"))
                pe.wait_ge(act_s, t.at((tag, "kept")))

            def nsa_pe(s, tag):
                u, T = s["u"], s["T"]
                for n in range(4):
                    pe.wait_ge(lo_done, u + n + 1)
                    for q in range(2):
                        if n >= 2:
                            pe.wait_ge(act_s, t.at((tag, "ev", n - 2, q)))
                        ins = cols_product(bank[2 * (n % 2) + q], (u + n) % RING, q, T, tag if n == 0 and q == 0 else None)
                        if q:
                            ins.then_inc(w_used, 1)
                        else:
                            t.done(ins, pe_s, (tag, "pu", n))
                pe.wait_ge(lo_done, u + 5)
                pe.wait_ge(act_s, t.at((tag, "ev", 2, 0)))
                for tt in range(2):
                    ins = rows_product(s, tag, bank[0][:, 48 * tt:48 * tt + 48], (u + 4) % RING, tt, 48, False)
                ins.then_inc(w_used, 1)
                pe.wait_ge(act_s, t.at((tag, "ev", 3, 1)))
                pe.wait_ge(act_s, t.at((tag, "gexp")))
                jobs = nsa_jobs
                for J in range(len(jobs) + 3):
                    if J < len(jobs):
                        g, tt, br, nk = jobs[J]
                        if J >= 2:
                            pe.wait_ge(dve_s, t.at((tag, "bias", J - 2)))
                        for r in range(R):
                            half, c = 64 * (r % 2), 2 * g + r // 2
                            keys = kcT[half:half + 64, g * N_CMP:(g + 1) * N_CMP] if br == 0 else kT[half:half + 64, br - 1, g, 0:nk]
                            ins = m.matmul(bank[2 * (J % 2) + r % 2][:, r // 2 * 256:r // 2 * 256 + nk],
                                           qT[half:half + 64, c, tt * P:(tt + 1) * P], keys, start=True, stop=True)
                        t.done(ins, pe_s, (tag, "s", J))
                    if 0 <= J - 2 < len(jobs):
                        i = J - 2
                        g, tt, br, nk = jobs[i]
                        pe.wait_ge(dve_s, t.at((tag, "p", i)))
                        if i:
                            pe.wait_ge(act_s, t.at((tag, "evT", i - 1)))
                        for kt in range(1 if br == 0 else tt + 1):
                            w = min(P, nk - kt * P)
                            for r in range(R):
                                ins = m.transpose(bank[4 + kt][0:w, r * P:(r + 1) * P], probs[i % 2][:, r, kt * P:kt * P + w], ident[:, :])
                        t.done(ins, pe_s, (tag, "jt", i))
                    if 0 <= J - 3:
                        i = J - 3
                        g, tt, br, nk = jobs[i]
                        ob = bank[6 + (i // 3) % 2][0:64, :]
                        if i >= 6 and i % 3 == 0:
                            pe.wait_ge(act_s, t.at((tag, "evO", i - 4)))
                        pe.wait_ge(act_s, t.at((tag, "evT", i)))
                        if br == 0:
                            ins = m.matmul(ob, vc[0:N_CMP, g * DH:(g + 1) * DH], pT[i % 2][0:N_CMP, 0, :], start=False, stop=True)
                        else:
                            for kt in range(tt + 1):
                                ins = m.matmul(ob, vn[:, br - 1, kt, g * DH:(g + 1) * DH], pT[i % 2][:, kt, :],
                                               start=(br == 1 and kt == 0), stop=False)
                        t.done(ins, pe_s, (tag, "pv", i))
                pe.wait_ge(act_s, t.at((tag, "evO", len(jobs) - 1)))
                pe.wait_ge(act_s, t.at((tag, "evO", len(jobs) - 4)))

            def wide_pe(s, tag):
                w, u = Wide(s), s["u"]
                for n in range(s["units"] + 1):
                    if n < s["units"]:
                        pe.wait_ge(lo_done, u + n + 1)
                        nt = w.tiles(n)
                        for tt in range(nt):
                            half = tt // 2
                            if n >= 2 and tt % 2 == 0 and half < w.tiles(n - 2) // 2:
                                pe.wait_ge(act_s, t.at((tag, "ev", n - 2, half)))
                            ins = rows_product(s, tag, bank[2 * (n % 2) + half][:, tt % 2 * WCOL:(tt % 2 + 1) * WCOL],
                                               (u + n) % RING, tt, WCOL, n == 0 and tt == 0)
                            if tt == nt - 1:
                                ins.then_inc(w_used, 1)
                            elif tt == 1:
                                t.done(ins, pe_s, (tag, "pu", n))
                    i = n - 1
                    if 0 <= i < w.nk:
                        pe.wait_ge(dve_s, t.at((tag, "rope", i)))
                        if i:
                            pe.wait_ge(act_s, t.at((tag, "evu", i - 1)))
                        for c in range(2):
                            for tt in range(w.tiles(i)):
                                o = tt * WCOL + c * P
                                ins = m.transpose(bank[4 + c][:, tt * P:(tt + 1) * P], w.nat(i)[:, o:o + P], ident[:, :])
                        t.done(ins, pe_s, (tag, "ut", i))
                n = s["units"] - 1
                for k in (n - 1, n):
                    pe.wait_ge(act_s, t.at((tag, "ev", k, 1)))
                pe.wait_ge(act_s, t.at((tag, "evu", w.nk - 1)))
                jobs = diff_jobs if w.diff else gqa_jobs
                for J in range(len(jobs) + 3):
                    if J < len(jobs):
                        h, tt, k0 = jobs[J]
                        b = J % 2
                        if J >= 2:
                            pe.wait_ge(act_s, t.at((tag, "exp", J - 2)))
                        if w.diff:
                            for m_ in range(2):
                                r = slice(64 * m_, 64 * m_ + 64)
                                ins = m.matmul(bank[2 * b + m_][:, 0:(4 - k0) * P], w.qT[r, h, tt * P:(tt + 1) * P],
                                               w.kT[r, h, k0 * P:512], start=True, stop=True)
                        else:
                            ins = m.matmul(bank[b][:, :], w.qT[:, h, tt * P:(tt + 1) * P], w.kT[:, h // 4, :], start=True, stop=True)
                        t.done(ins, pe_s, (tag, "s", J))
                    if 0 <= J - 2 < len(jobs):
                        i = J - 2
                        h, tt, k0 = jobs[i]
                        src, dst = (probs_d[i % 2][0], bank[4 + i % 2]) if w.diff else (probs_g[i % 2], bank[2 + i % 2])
                        pe.wait_ge(dve_s, t.at((tag, "p", i)))
                        if i >= 2:
                            pe.wait_ge(act_s, t.at((tag, "evT", i - 2)))
                        for kt in range(4 - k0):
                            ins = m.transpose(dst[:, kt * P:(kt + 1) * P], src[:, kt * P:(kt + 1) * P], ident[:, :])
                        t.done(ins, pe_s, (tag, "jt", i))
                    if 0 <= J - 3:
                        i = J - 3
                        h, tt, k0 = jobs[i]
                        if h >= 2 and tt == 0:
                            pe.wait_ge(act_s, t.at((tag, "evO", h - 2)))
                        pe.wait_ge(act_s, t.at((tag, "evT", i)))
                        for kt in range(4 - k0):
                            fl = dict(start=(kt == 0), stop=(kt == 3 - k0))
                            if w.diff:
                                ins = m.matmul(bank[6 + h % 2][:, tt * P:(tt + 1) * P], aT_d[i % 2][:, kt * P:(kt + 1) * P],
                                               w.v[:, k0 + kt, h * P:(h + 1) * P], **fl)
                            else:
                                ins = m.matmul(bank[4 + h % 2][:, tt * P:(tt + 1) * P], w.v[:, kt, h // 4 * P:(h // 4 + 1) * P],
                                               pT_g[i % 2][:, kt * P:(kt + 1) * P], **fl)
                        t.done(ins, pe_s, (tag, "pv", i))
                if w.diff:
                    for h in range(8):
                        pe.wait_ge(dve_s, t.at((tag, "on", h)))
                        if h >= 4:
                            pe.wait_ge(act_s, t.at((tag, "evo", h - 4)))
                        for tt in range(4):
                            ins = m.transpose(bank[h % 4][:, tt * P:(tt + 1) * P], w.qT[:, h, tt * P:(tt + 1) * P], ident[:, :])
                        t.done(ins, pe_s, (tag, "ot", h))
                    t.marks[("ada", "free")] = t.now["pe_s"]
                pe.wait_ge(act_s, t.at((tag, "o")))

            pe.wait_ge(rows_landed, t.at("small_rows"))
            pe.wait_ge(pool_s, t.at("ident"))
            for b in range((ncol + P - 1) // P):
                rows = min(P, ncol - b * P)
                ins = m.transpose(bank[0][:, b * P:b * P + rows], diag[0:rows, 0, b * P:(b + 1) * P], ident[0:rows, 0:rows])
            t.done(ins, pe_s, "cols_t")
            pe.wait_ge(act_s, t.at("cond"))
            pe.wait_ge(pool_s, t.at(("sel", 3, 1)))
            for vi in range(3):
                vec_acc(vi, 0)
                vec_acc(vi, 1)
                vec_sum(vi)
            for si, s in enumerate(subs):
                tag = f"s{si}"
                if si == 0:
                    pe.wait_ge(dve_s, t.at("cols"))
                    pe.wait_ge(ada_col, 3)
                prep(s, tag)
                u, c, T = s["u"], s["c"], s["T"]

                def up_step(j, i, parts, banks, first, also=None):
                    k = 0 if i is None else i * 3
                    for part in range(parts):
                        n = u + parts * j + part
                        pe.wait_ge(lo_done, n + 1 + k * parts)
                        for q in range(2):
                            if s["kind"] == "ffn":
                                if part == 0 and (s["sc"] + 2 * j + q >= 2 or i is not None):
                                    pe.wait_ge(silu_done, s["sc"] + 2 * j + q - 1 + 2 * k)
                                if part == 1 and (c + 2 * j + q >= 2 or i is not None):
                                    pe.wait_ge(mid_done, c + 2 * j + q - 1 + 2 * k)
                            elif j:
                                if part < 2:
                                    pe.wait_ge(dve_s, t.at((tag, "v", 2 * (j - 1) + q)))
                                else:
                                    pe.wait_ge(mid_done, c + 2 * (j - 1) + q + 1)
                            ins = cols_product(bank[banks[part] + q], n % RING, q, T,
                                               tag if first and part == 0 and q == 0 else None)
                            ins.then_inc(w_used if q else part_done[part], 1)
                            if also:
                                for f in also.get((part, q), ()):
                                    f()

                early = s["kind"] == "ffn" and T == 256
                if s["kind"] == "ffn":
                    def block3(j0, i):
                        for j in range(3):
                            if j < 2 and s["nvec"]:
                                vec_acc(s["v"], j, i)
                            up_step(j, i, 2, (0, 2), i is None and j == 0)
                        if s["nvec"]:
                            vec_sum(s["v"], i)
                    for_steps(pe, s, block3)
                    v9, v10 = s["v"] + 3, s["v"] + 4
                    also = {}
                    if s["nvec"]:
                        vec_acc(v9, 0)
                    up_step(9, None, 2, (0, 2), False)
                    if s["nvec"]:
                        vec_acc(v9, 1)
                        also[0, 1] = (lambda: vec_sum(v9), lambda: vec_acc(v10, 0))
                    if early:
                        also[1, 0] = (lambda: gates(s, tag),)
                    up_step(10, None, 2, (0, 2), False, also)
                    if s["nvec"] and not early:
                        vec_acc(v10, 1)
                        vec_sum(v10)
                elif s["kind"] == "conv":
                    for j in range(4):
                        if j:
                            up_step(j, None, 3, (0, 2, 6), False, {(0, 1): (lambda: vec_sum(s["v"] + j - 1),),
                                                                   (1, 0): (lambda: vec_acc(s["v"] + j, 0),)})
                        else:
                            vec_acc(s["v"], 0)
                            up_step(j, None, 3, (0, 2, 6), True)
                        vec_acc(s["v"] + j, 1)
                    vec_sum(s["v"] + 3)
                    pe.wait_ge(mid_done, c + 8)
                elif s["kind"] == "kv":
                    kv_pe(s, tag)
                    continue
                elif s["kind"] == "nsa":
                    nsa_pe(s, tag)
                elif s["kind"] in ("diff", "gqa"):
                    wide_pe(s, tag)
                if not early:
                    gates(s, tag)
                down(s, tag, s["v"] + 4 if early and s["nvec"] else None)
    return t


NAMES = ["x", "c", "ada_w", "ada_b", "norm_g", "ffn_w_in", "ffn_w_out", "a_w_in", "a_conv", "a_w_out", "kv_norm_g",
         "kv_ada_w", "kv_ada_b", "kv_w", "cmp_pos", "cmp_w1", "cmp_w2", "b_w_in", "b_w_out", "c_2", "ctx_2", "c_ctx_2",
         "ada_w_2", "ada_b_2", "norm1_g_2", "norm2_g_2", "ffn_w_gu_2", "ffn_w_down_2", "diff_w_in_2", "diff_w_out_2",
         "diff_q_norm_2", "diff_k_norm_2", "diff_lambda_q1_2", "diff_lambda_k1_2", "diff_lambda_q2_2",
         "diff_lambda_k2_2", "diff_subln_2", "gqa_w_in_2", "gqa_w_out_2", "gqa_q_norm_2", "gqa_k_norm_2"]
STOP = None


def rope(dh):
    token = np.arange(SEQ)
    half = dh // 2
    inv = np.float32(10000.0) ** (-np.arange(0, half, 2, dtype=np.float32) / np.float32(half))
    axes = [pos.astype(np.float32)[:, None] * inv[None, :] for pos in (token // GRID_W, token % GRID_W)]
    ang = np.concatenate([axes[0], axes[0], axes[1], axes[1]], axis=-1)
    return np.stack([np.cos(ang), np.sin(ang)]).astype(np.float32)


def program(nc, shapes, marks):
    io = {n: nc.dram_tensor(f"in_{n}", shapes[n], F32, kind="ExternalInput").ap() for n in NAMES + ["rope64", "rope128"]}
    out = nc.dram_tensor("out_0", (1, SEQ, D), F32, kind="ExternalOutput").ap()
    return trace(nc, Tally(marks), io, out, STOP).marks


def kernel(**inputs):
    import concourse.bacc as bacc
    from concourse.bass_utils import run_bass_kernel_spmd

    arrays = {f"in_{n}": np.ascontiguousarray(inputs[n]) for n in NAMES}
    for dh in (64, 128):
        arrays[f"in_rope{dh}"] = rope(dh)
    shapes = {n[3:]: a.shape for n, a in arrays.items()}
    marks = program(bacc.Bacc("TRN2", target_bir_lowering=False, num_devices=1), shapes, None)
    nc = bacc.Bacc("TRN2", target_bir_lowering=False, num_devices=1)
    program(nc, shapes, marks)
    r = run_bass_kernel_spmd(nc, [arrays], core_ids=[0])
    return r.results[0]["out_0"]
```
